# Optimizing a Trainium2 kernel written in Bass

```python
import math
import jax, jax.numpy as jnp
from jax import lax
import numpy as np

D_MODEL = 1024
BATCH = 1
SEQ = 512
DEPTH = 2

N_MIXERS = 2
N_ATTN_LAYERS = (DEPTH + 1) // 2
N_POOL_LAYERS = DEPTH // 2
N_HEADS = 8
HEAD_DIM = D_MODEL // (2 * N_HEADS)
V_DIM = 2 * HEAD_DIM
QK_WIDTH = 2 * N_HEADS * HEAD_DIM
ROT_DIM = HEAD_DIM // 4
ROPE_THETA = 500000.0
Q_BLOCK = 128
SUBLN_EPS = 1e-5
POOL_WINDOWS = (2, 4, 8, 16)
N_POOL_GROUPS = len(POOL_WINDOWS)
POOL_GROUP_DIM = D_MODEL // N_POOL_GROUPS
N_GROUPS = 4
EXPERTS_PER_GROUP = 8
N_EXPERTS = N_GROUPS * EXPERTS_PER_GROUP
TOP_K = 2
D_EXPERT = D_MODEL // 2
MOE_BLOCK = 128
ROUTER_BIAS_SCALE = 0.01
DEEPNORM_ALPHA = (2 * DEPTH) ** 0.25
DEEPNORM_BETA = (8 * DEPTH) ** -0.25
LN_EPS = 1e-5


def layer_norm(x, g, b):
    xf = x.astype(jnp.float32)
    mu = jnp.mean(xf, -1, keepdims=True)
    var = jnp.mean(jnp.square(xf - mu), -1, keepdims=True)
    return ((xf - mu) * lax.rsqrt(var + LN_EPS) * g + b).astype(x.dtype)

def rotary_tables(seq):
    inv = ROPE_THETA ** (-jnp.arange(0, ROT_DIM, 2, dtype=jnp.float32) / ROT_DIM)
    ang = jnp.arange(seq, dtype=jnp.float32)[:, None] * inv[None, :]
    return jnp.cos(ang), jnp.sin(ang)

def apply_partial_rope(t, cos, sin):
    half = ROT_DIM // 2
    shape = (1, cos.shape[0]) + (1,) * (t.ndim - 3) + (half,)
    c = cos.reshape(shape).astype(t.dtype)
    s = sin.reshape(shape).astype(t.dtype)
    r1, r2, rest = t[..., :half], t[..., half:ROT_DIM], t[..., ROT_DIM:]
    return jnp.concatenate([r1 * c - r2 * s, r1 * s + r2 * c, rest], axis=-1)

def diff_attention(x, w_qkv, w_o, lq1, lk1, lq2, lk2, sub_g, lambda_init, cos, sin):
    B, S, _ = x.shape
    qkv = x @ w_qkv
    q, k, v = jnp.split(qkv, [QK_WIDTH, 2 * QK_WIDTH], axis=-1)
    q = apply_partial_rope(q.reshape(B, S, N_HEADS, 2, HEAD_DIM), cos, sin)
    k = apply_partial_rope(k.reshape(B, S, N_HEADS, 2, HEAD_DIM), cos, sin)
    q = q.transpose(0, 2, 3, 1, 4)
    k = k.transpose(0, 2, 3, 1, 4)
    v = v.reshape(B, S, N_HEADS, V_DIM).transpose(0, 2, 1, 3)
    lam = (jnp.exp(jnp.sum(lq1 * lk1).astype(jnp.float32))
           - jnp.exp(jnp.sum(lq2 * lk2).astype(jnp.float32)) + lambda_init)
    scale = HEAD_DIM ** -0.5
    outs = []
    for blk in range(S // Q_BLOCK):
        lo, hi = blk * Q_BLOCK, (blk + 1) * Q_BLOCK
        qb = q[:, :, :, lo:hi]
        kb = k[:, :, :, :hi]
        vb = v[:, :, :hi]
        s = jnp.einsum('bhmqd,bhmkd->bhmqk', qb, kb).astype(jnp.float32) * scale
        mask = jnp.arange(lo, hi)[:, None] >= jnp.arange(hi)[None, :]
        p = jax.nn.softmax(jnp.where(mask, s, -jnp.inf), axis=-1)
        a = (p[:, :, 0] - lam * p[:, :, 1]).astype(v.dtype)
        outs.append(jnp.einsum('bhqk,bhkd->bhqd', a, vb))
    o = jnp.concatenate(outs, axis=2).astype(jnp.float32)
    o = o * lax.rsqrt(jnp.mean(jnp.square(o), -1, keepdims=True) + SUBLN_EPS) * sub_g
    o = (o * (1.0 - lambda_init)).astype(x.dtype)
    o = o.transpose(0, 2, 1, 3).reshape(B, S, N_HEADS * V_DIM)
    return o @ w_o

def pool_mixer(x, w_in, w_grp, ls, w_out):
    B, S, _ = x.shape
    u = (x @ w_in).reshape(B, S, N_POOL_GROUPS, POOL_GROUP_DIM)
    count = jnp.arange(1, S + 1, dtype=jnp.float32)
    feats = []
    for g, w in enumerate(POOL_WINDOWS):
        ug = u[:, :, g].astype(jnp.float32)
        cs = jnp.cumsum(ug, axis=1)
        lag = jnp.pad(cs[:, :S - w], ((0, 0), (w, 0), (0, 0)))
        mean = (cs - lag) / jnp.minimum(count, float(w))[None, :, None]
        feats.append(mean - ug)
    p = jnp.stack(feats, axis=2).astype(x.dtype)
    y = jnp.einsum('bsgc,gcd->bsgd', p, w_grp).reshape(B, S, D_MODEL) * ls
    return y @ w_out

def hier_moe(x, w_grp_router, b_grp_router, w_exp_router, b_exp_router, w_gate, w_up, w_down):
    B, S, D = x.shape
    N = B * S
    xf = x.reshape(N, D)
    g_logits = (xf @ w_grp_router + b_grp_router).astype(jnp.float32)
    g_idx = jnp.argmax(g_logits, axis=-1)
    g_p = jnp.take_along_axis(jax.nn.softmax(g_logits, -1), g_idx[:, None], -1)
    e_logits = (xf @ w_exp_router + b_exp_router).astype(jnp.float32)
    e_logits = e_logits.reshape(N, N_GROUPS, EXPERTS_PER_GROUP)
    e_in = jnp.take_along_axis(e_logits, g_idx[:, None, None], axis=1)[:, 0]
    top_v, top_i = lax.top_k(e_in, TOP_K)
    gate = g_p * jax.nn.softmax(top_v, axis=-1)
    expert_id = g_idx[:, None] * EXPERTS_PER_GROUP + top_i
    A = N * TOP_K
    eid = expert_id.reshape(A)
    tok = jnp.repeat(jnp.arange(N, dtype=jnp.int32), TOP_K)
    wts = gate.reshape(A)
    order = jnp.argsort(eid)
    eid_s, tok_s, w_s = eid[order], tok[order], wts[order]
    counts = jnp.bincount(eid, length=N_EXPERTS)
    starts = jnp.cumsum(counts) - counts
    padded = (counts + MOE_BLOCK - 1) // MOE_BLOCK * MOE_BLOCK
    pad_ends = jnp.cumsum(padded)
    pad_starts = pad_ends - padded
    dest = pad_starts[eid_s] + jnp.arange(A) - starts[eid_s]
    P = A + N_EXPERTS * MOE_BLOCK
    NB = P // MOE_BLOCK
    tok_pad = jnp.zeros((P,), jnp.int32).at[dest].set(tok_s)
    w_pad = jnp.zeros((P,), wts.dtype).at[dest].set(w_s)
    blk_e = jnp.minimum(jnp.searchsorted(pad_ends, jnp.arange(NB) * MOE_BLOCK, side='right'),
                        N_EXPERTS - 1)
    xin = xf[tok_pad].reshape(NB, MOE_BLOCK, D)

    def run_block(args):
        xb, e = args
        h = jax.nn.silu(xb @ w_gate[e]) * (xb @ w_up[e])
        return h @ w_down[e]

    y = lax.map(run_block, (xin, blk_e)).reshape(P, D)
    out = jnp.zeros((N, D), x.dtype).at[tok_pad].add(y * w_pad[:, None].astype(y.dtype))
    return out.reshape(B, S, D)

def first_inputs(seed: int = 0) -> dict:
    key = jax.random.key(seed)
    ks = jax.random.split(key, 24)
    f32 = jnp.float32
    nrm = lambda k, shp, sc: jax.random.normal(k, shp, f32) * sc
    D = D_MODEL
    w_qk = nrm(ks[1], (N_ATTN_LAYERS, D, 2 * QK_WIDTH), D ** -0.5)
    w_v = nrm(ks[2], (N_ATTN_LAYERS, D, N_HEADS * V_DIM), D ** -0.5) * DEEPNORM_BETA
    return {
        "x": jax.random.normal(ks[0], (BATCH, SEQ, D), f32),
        "attn_w_qkv": jnp.concatenate([w_qk, w_v], axis=-1),
        "attn_w_o": nrm(ks[3], (N_ATTN_LAYERS, N_HEADS * V_DIM, D), (N_HEADS * V_DIM) ** -0.5) * DEEPNORM_BETA,
        "attn_lq1": nrm(ks[4], (N_ATTN_LAYERS, HEAD_DIM), 0.1),
        "attn_lk1": nrm(ks[5], (N_ATTN_LAYERS, HEAD_DIM), 0.1),
        "attn_lq2": nrm(ks[6], (N_ATTN_LAYERS, HEAD_DIM), 0.1),
        "attn_lk2": nrm(ks[7], (N_ATTN_LAYERS, HEAD_DIM), 0.1),
        "attn_sub_g": 1.0 + nrm(ks[8], (N_ATTN_LAYERS, V_DIM), 0.02),
        "pool_w_in": nrm(ks[9], (N_POOL_LAYERS, D, D), D ** -0.5),
        "pool_w_grp": nrm(ks[10], (N_POOL_LAYERS, N_POOL_GROUPS, POOL_GROUP_DIM, POOL_GROUP_DIM), POOL_GROUP_DIM ** -0.5),
        "pool_scale": 1.0 + nrm(ks[11], (N_POOL_LAYERS, D), 0.02),
        "pool_w_out": nrm(ks[12], (N_POOL_LAYERS, D, D), D ** -0.5) * DEEPNORM_BETA,
        "ln_g": 1.0 + nrm(ks[13], (DEPTH, 2, D), 0.02),
        "ln_b": nrm(ks[14], (DEPTH, 2, D), 0.02),
        "moe_w_grp_router": nrm(ks[15], (DEPTH, D, N_GROUPS), D ** -0.5),
        "moe_b_grp_router": nrm(ks[16], (DEPTH, N_GROUPS), ROUTER_BIAS_SCALE),
        "moe_w_exp_router": nrm(ks[17], (DEPTH, D, N_EXPERTS), D ** -0.5),
        "moe_b_exp_router": nrm(ks[18], (DEPTH, N_EXPERTS), ROUTER_BIAS_SCALE),
        "moe_w_gate": nrm(ks[19], (DEPTH, N_EXPERTS, D, D_EXPERT), D ** -0.5),
        "moe_w_up": nrm(ks[20], (DEPTH, N_EXPERTS, D, D_EXPERT), D ** -0.5),
        "moe_w_down": nrm(ks[21], (DEPTH, N_EXPERTS, D_EXPERT, D), D_EXPERT ** -0.5) * DEEPNORM_BETA,
    }

def first_block(x, attn_w_qkv, attn_w_o, attn_lq1, attn_lk1, attn_lq2, attn_lk2, attn_sub_g,
              pool_w_in, pool_w_grp, pool_scale, pool_w_out, ln_g, ln_b,
              moe_w_grp_router, moe_b_grp_router, moe_w_exp_router, moe_b_exp_router,
              moe_w_gate, moe_w_up, moe_w_down):
    cos, sin = rotary_tables(x.shape[1])
    h = x
    for i in range(DEPTH):
        j = i // N_MIXERS
        if i % N_MIXERS == 0:
            lambda_init = 0.8 - 0.6 * math.exp(-0.3 * i)
            mix = diff_attention(h, attn_w_qkv[j], attn_w_o[j], attn_lq1[j], attn_lk1[j],
                                 attn_lq2[j], attn_lk2[j], attn_sub_g[j], lambda_init, cos, sin)
        else:
            mix = pool_mixer(h, pool_w_in[j], pool_w_grp[j], pool_scale[j], pool_w_out[j])
        h = layer_norm(DEEPNORM_ALPHA * h + mix, ln_g[i, 0], ln_b[i, 0])
        ffn = hier_moe(h, moe_w_grp_router[i], moe_b_grp_router[i], moe_w_exp_router[i],
                       moe_b_exp_router[i], moe_w_gate[i], moe_w_up[i], moe_w_down[i])
        h = layer_norm(DEEPNORM_ALPHA * h + ffn, ln_g[i, 1], ln_b[i, 1])
    return h


DEPTH_2 = 1

CHUNK = 64
ATT_HEADS = 8
HEAD_DIM_2 = 64
ATT_WIDTH = ATT_HEADS * HEAD_DIM_2
LRU_WIDTH = D_MODEL - ATT_WIDTH
LRU_BLOCKS = 8
LRU_BLOCK_DIM = LRU_WIDTH // LRU_BLOCKS
CONV_WIDTH = 4
LRU_C = 8.0
TOP_K_INNER = 2
D_EXPERT_2 = 256
RMS_EPS = 1e-6
IN_SIZES = (ATT_WIDTH, ATT_WIDTH, ATT_WIDTH, ATT_HEADS, LRU_WIDTH, LRU_WIDTH)
IN_COLS = sum(IN_SIZES)


def rmsnorm(x, g):
    xf = x.astype(jnp.float32)
    inv = lax.rsqrt(jnp.mean(xf * xf, axis=-1, keepdims=True) + RMS_EPS)
    return (xf * inv * g.astype(jnp.float32)).astype(x.dtype)

def forgetting_attention(q, k, v, log_f):
    b, s, h, dh = q.shape
    c = jnp.cumsum(log_f, axis=1).transpose(0, 2, 1)
    n_blk = s // Q_BLOCK
    q_blk = q.reshape(b, n_blk, Q_BLOCK, h, dh).transpose(1, 0, 2, 3, 4)
    c_blk = c.reshape(b, h, n_blk, Q_BLOCK).transpose(2, 0, 1, 3)
    starts = jnp.arange(n_blk, dtype=jnp.int32) * Q_BLOCK
    k_pos = jnp.arange(s, dtype=jnp.int32)
    scale = HEAD_DIM_2 ** -0.5

    def one_block(args):
        qb, cb, start = args
        logits = jnp.einsum('bqhd,bkhd->bhqk', qb, k, preferred_element_type=jnp.float32) * scale
        decay = cb[..., :, None] - c[..., None, :]
        q_pos = start + jnp.arange(Q_BLOCK, dtype=jnp.int32)
        causal = k_pos[None, :] <= q_pos[:, None]
        logits = jnp.where(causal, logits + decay, -1e30)
        p = jax.nn.softmax(logits, axis=-1)
        return jnp.einsum('bhqk,bkhd->bqhd', p.astype(v.dtype), v)

    out = lax.map(one_block, (q_blk, c_blk, starts))
    return out.transpose(1, 0, 2, 3, 4).reshape(b, s, h * dh)

def causal_depthwise_conv(x, w, bias):
    s = x.shape[1]
    xp = jnp.pad(x, ((0, 0), (CONV_WIDTH - 1, 0), (0, 0)))
    out = bias + w[0] * xp[:, 0:s]
    for tap in range(1, CONV_WIDTH):
        out = out + w[tap] * xp[:, tap:tap + s]
    return out

def block_diag_linear(x, w, b):
    xb = x.reshape(x.shape[:-1] + (LRU_BLOCKS, LRU_BLOCK_DIM))
    y = jnp.einsum('bsni,nij->bsnj', xb, w) + b
    return y.reshape(x.shape)

def rg_lru(x, w_a, b_a, w_x, b_x, lam):
    r = jax.nn.sigmoid(block_diag_linear(x, w_a, b_a)).astype(jnp.float32)
    i = jax.nn.sigmoid(block_diag_linear(x, w_x, b_x))
    log_a = -LRU_C * r * jax.nn.softplus(-lam.astype(jnp.float32))
    a = jnp.exp(log_a)
    mult = jnp.sqrt(-jnp.expm1(2.0 * log_a))
    u = mult * (i * x).astype(jnp.float32)

    def combine(left, right):
        a_l, u_l = left
        a_r, u_r = right
        return a_r * a_l, a_r * u_l + u_r

    _, hseq = lax.associative_scan(combine, (a, u), axis=1)
    return hseq.astype(x.dtype)

def hierarchical_moe(t, w_group, b_group, w_inner, b_inner, w_gate, w_up, w_down):
    group_p = jax.nn.softmax((t @ w_group + b_group).astype(jnp.float32), axis=-1)
    g_w, g_idx = lax.top_k(group_p, 1)
    inner_all = jnp.einsum('nd,gde->nge', t, w_inner) + b_inner
    inner_logits = jnp.take_along_axis(inner_all, g_idx[:, :, None], axis=1)[:, 0]
    inner_p = jax.nn.softmax(inner_logits.astype(jnp.float32), axis=-1)
    e_w, e_idx = lax.top_k(inner_p, TOP_K_INNER)
    e_w = e_w / jnp.sum(e_w, axis=-1, keepdims=True)
    expert_w = jnp.sum(jax.nn.one_hot(e_idx, EXPERTS_PER_GROUP, dtype=jnp.float32) * e_w[..., None], axis=1)
    combine = (g_w[:, :, None]
               * jax.nn.one_hot(g_idx[:, 0], N_GROUPS, dtype=jnp.float32)[:, :, None]
               * expert_w[:, None, :]).astype(t.dtype)
    y = jnp.zeros_like(t)
    for g in range(N_GROUPS):
        hg = jax.nn.silu(jnp.einsum('nd,edf->nef', t, w_gate[g])) * jnp.einsum('nd,edf->nef', t, w_up[g])
        y = y + jnp.einsum('nef,efd->nd', hg * combine[:, g, :, None], w_down[g])
    return y

def second_inputs(seed: int = 0) -> dict:
    key = jax.random.key(seed)
    ks = jax.random.split(key, 24)
    nrm = jax.random.normal
    L, D, G, E, F = DEPTH_2, D_MODEL, N_GROUPS, EXPERTS_PER_GROUP, D_EXPERT_2
    a0 = jax.random.uniform(ks[10], (L, LRU_WIDTH), minval=0.9, maxval=0.999)
    sig = a0 ** (1.0 / LRU_C)
    lam = jnp.log(sig) - jnp.log1p(-sig)
    return {
        'x': nrm(ks[0], (BATCH, SEQ, D), jnp.float32),
        'mix_norm': 1.0 + 0.05 * nrm(ks[1], (L, D), jnp.float32),
        'w_in': nrm(ks[2], (L, D, IN_COLS), jnp.float32) * D ** -0.5,
        'b_forget': jnp.linspace(1.0, 6.0, ATT_HEADS, dtype=jnp.float32) + 0.1 * nrm(ks[3], (L, ATT_HEADS), jnp.float32),
        'conv_w': nrm(ks[4], (L, CONV_WIDTH, LRU_WIDTH), jnp.float32) * CONV_WIDTH ** -0.5,
        'conv_b': 0.02 * nrm(ks[5], (L, LRU_WIDTH), jnp.float32),
        'w_a': nrm(ks[6], (L, LRU_BLOCKS, LRU_BLOCK_DIM, LRU_BLOCK_DIM), jnp.float32) * LRU_BLOCK_DIM ** -0.5,
        'b_a': 0.02 * nrm(ks[7], (L, LRU_BLOCKS, LRU_BLOCK_DIM), jnp.float32),
        'w_x': nrm(ks[8], (L, LRU_BLOCKS, LRU_BLOCK_DIM, LRU_BLOCK_DIM), jnp.float32) * LRU_BLOCK_DIM ** -0.5,
        'b_x': 0.02 * nrm(ks[9], (L, LRU_BLOCKS, LRU_BLOCK_DIM), jnp.float32),
        'lru_lambda': lam,
        'w_out': nrm(ks[11], (L, D, D), jnp.float32) * D ** -0.5,
        'ffn_norm': 1.0 + 0.05 * nrm(ks[12], (L, D), jnp.float32),
        'w_group': nrm(ks[13], (L, D, G), jnp.float32) * D ** -0.5,
        'b_group': 0.01 * nrm(ks[14], (L, G), jnp.float32),
        'w_inner': nrm(ks[15], (L, G, D, E), jnp.float32) * D ** -0.5,
        'b_inner': 0.01 * nrm(ks[16], (L, G, E), jnp.float32),
        'w_gate': nrm(ks[17], (L, G, E, D, F), jnp.float32) * D ** -0.5,
        'w_up': nrm(ks[18], (L, G, E, D, F), jnp.float32) * D ** -0.5,
        'w_down': nrm(ks[19], (L, G, E, F, D), jnp.float32) * F ** -0.5,
        'final_norm': 1.0 + 0.05 * nrm(ks[20], (D,), jnp.float32),
    }

def second_block(x, mix_norm, w_in, b_forget, conv_w, conv_b, w_a, b_a, w_x, b_x, lru_lambda,
              w_out, ffn_norm, w_group, b_group, w_inner, b_inner, w_gate, w_up, w_down, final_norm):
    b, s, d = x.shape
    split_points = [int(v) for v in np.cumsum(IN_SIZES)[:-1]]
    for l in range(DEPTH_2):
        h = rmsnorm(x, mix_norm[l])
        z = h @ w_in[l]
        q, k, v, f_logit, gate_in, rec_in = jnp.split(z, split_points, axis=-1)
        log_f = jax.nn.log_sigmoid(f_logit.astype(jnp.float32) + b_forget[l].astype(jnp.float32))
        att = forgetting_attention(q.reshape(b, s, ATT_HEADS, HEAD_DIM_2),
                                   k.reshape(b, s, ATT_HEADS, HEAD_DIM_2),
                                   v.reshape(b, s, ATT_HEADS, HEAD_DIM_2), log_f)
        rec = causal_depthwise_conv(rec_in, conv_w[l], conv_b[l])
        rec = rg_lru(rec, w_a[l], b_a[l], w_x[l], b_x[l], lru_lambda[l])
        lru_out = rec * jax.nn.gelu(gate_in, approximate=True)
        x = x + jnp.concatenate([att, lru_out], axis=-1) @ w_out[l]
        h2 = rmsnorm(x, ffn_norm[l]).reshape(b * s, d)
        y = hierarchical_moe(h2, w_group[l], b_group[l], w_inner[l], b_inner[l],
                             w_gate[l], w_up[l], w_down[l])
        x = x + y.reshape(b, s, d)
    return rmsnorm(x, final_norm)


def setup_inputs(seed=0):
    out = dict(first_inputs(seed))
    for name, value in second_inputs(seed + 1).items():
        if name != "x":
            out[name + "_2"] = value
    return out


def reference(
    x, attn_w_qkv, attn_w_o, attn_lq1, attn_lk1, attn_lq2, attn_lk2, attn_sub_g, pool_w_in,
    pool_w_grp, pool_scale, pool_w_out, ln_g, ln_b, moe_w_grp_router, moe_b_grp_router,
    moe_w_exp_router, moe_b_exp_router, moe_w_gate, moe_w_up, moe_w_down, mix_norm_2, w_in_2,
    b_forget_2, conv_w_2, conv_b_2, w_a_2, b_a_2, w_x_2, b_x_2, lru_lambda_2, w_out_2,
    ffn_norm_2, w_group_2, b_group_2, w_inner_2, b_inner_2, w_gate_2, w_up_2, w_down_2,
    final_norm_2,
):
    x = first_block(
        x, attn_w_qkv, attn_w_o, attn_lq1, attn_lk1, attn_lq2, attn_lk2, attn_sub_g, pool_w_in,
        pool_w_grp, pool_scale, pool_w_out, ln_g, ln_b, moe_w_grp_router, moe_b_grp_router,
        moe_w_exp_router, moe_b_exp_router, moe_w_gate, moe_w_up, moe_w_down,
    )
    return second_block(
        x, mix_norm_2, w_in_2, b_forget_2, conv_w_2, conv_b_2, w_a_2, b_a_2, w_x_2, b_x_2,
        lru_lambda_2, w_out_2, ffn_norm_2, w_group_2, b_group_2, w_inner_2, b_inner_2, w_gate_2,
        w_up_2, w_down_2, final_norm_2,
    )


_drawn_inputs = setup_inputs


def setup_inputs(seed=0):
    import zlib

    import numpy as np

    out = dict(_drawn_inputs(seed))
    spreads = {}
    factors = {'pool_scale': 3.202,
     'moe_b_grp_router': 6.057,
     'moe_b_exp_router': 3.154,
     'b_a_2': 8.0,
     'b_x_2': 8.0,
     'b_group_2': 8.0,
     'b_inner_2': 4.156}
    for name, (base, spread) in spreads.items():
        noise = np.random.default_rng([zlib.crc32(name.encode()), seed]).standard_normal(out[name].shape)
        drawn = base * np.exp(spread * noise) if base else spread * noise
        out[name] = __import__('jax').numpy.asarray(drawn.astype(out[name].dtype))
    for name, factor in factors.items():
        out[name] = (out[name] * factor).astype(out[name].dtype)
    return out
```

```python
import concourse.bass as bass
from concourse import mybir
from contextlib import ExitStack

D = 1024
S = 512
P = 128
T = S // P
K = D // P
E = 32
NG = 4
BLK = 64
MAIN = 64
OVF = 15
UNITS = 12
UW = 2048
BIG = 1e30
ALPHA = 4.0 ** 0.25
LAMBDA_INIT = 0.8 - 0.6
FDIM = (512, 512, 256)

C_ID, C_TRI, C_ONE, C_CAUS, C_ROPE, C_IO, C_GRP, C_J, C_INV, C_TH, C_W = \
    0, 128, 256, 384, 512, 640, 672, 704, 720, 784, 792


def rank_thresholds():
    return [MAIN + BLK * k for k in range((S - MAIN + BLK - 1) // BLK)]


def weight_plan(w):
    units, first = [], {}

    def add(name, ap):
        first.setdefault(name, len(units))
        units.append(ap)

    def cols(name, ap, lo):
        add(name, ap[:, lo:lo + 256].rearrange("(k p) n -> p k n", p=P))

    def rows(name, ap, width):
        for n in range(width // 512):
            for kk in range(2):
                add(name, ap[512 * kk:512 * kk + 512, 512 * n:512 * n + 512].rearrange("(k p) n -> p k n", p=P))

    rows("v", w["qkv"][:, 2 * D:3 * D], D)
    for pair in range(4):
        cols("qk", w["qkv"], 256 * pair)
        cols("qk", w["qkv"], D + 256 * pair)
    rows("wo", w["wo"], D)
    first["moe0"] = len(units)
    units += [None] * (E * 6)
    for g in range(4):
        cols("pin", w["pin"], 256 * g)
    add("pgrp", w["pgrp"].rearrange("g (c p) n -> p (g c) n", p=P))
    rows("pout", w["pout"], D)
    first["moe1"] = len(units)
    units += [None] * (E * 6)
    for lo in (2056, 2312):
        cols("rec", w["in2"], lo)
    for lo in (1544, 1800):
        cols("gate", w["in2"], lo)
    for lo in (0, 256):
        cols("q2", w["in2"], lo)
    for lo in (512, 768):
        cols("k2", w["in2"], lo)
    rows("v2", w["in2"][:, 1024:1536], 512)
    rows("out2", w["out2"], D)
    first["moe2"] = len(units)
    return units, first


def program(nc, t):
    f32, u32 = mybir.dt.float32, mybir.dt.uint32
    ACT, ALU, AX = mybir.ActivationFunctionType, mybir.AluOpType, mybir.AxisListType.X
    w = {"qkv": t["attn_w_qkv"][0], "wo": t["attn_w_o"][0], "pin": t["pool_w_in"][0],
         "pgrp": t["pool_w_grp"][0], "pout": t["pool_w_out"][0], "in2": t["w_in_2"][0], "out2": t["w_out_2"][0]}
    units, first = weight_plan(w)
    experts = [[t[n][l] for n in ("moe_w_gate", "moe_w_up", "moe_w_down")] for l in range(2)]
    experts.append([t[n][0].rearrange("g e a b -> (g e) a b") for n in ("w_gate_2", "w_up_2", "w_down_2")])
    router_g = [t["moe_w_grp_router"][0], t["moe_w_grp_router"][1], t["w_group_2"][0]]
    router_gb = [t["moe_b_grp_router"][0:1], t["moe_b_grp_router"][1:2], t["b_group_2"][0:1]]
    router_eb = [t["moe_b_exp_router"][0:1], t["moe_b_exp_router"][1:2],
                 t["b_inner_2"].rearrange("l g e -> l (g e)")[0:1]]

    rows_ = (E + OVF + 2) * BLK
    rows_ += rows_ % P
    x_rows = nc.dram_tensor("x_rows", (rows_, D), f32, kind="Internal").ap()
    y_rows = nc.dram_tensor("y_rows", (rows_, D), f32, kind="Internal").ap()

    with ExitStack() as c:
        def sb(name, shape, dt=f32):
            return c.enter_context(nc.sbuf_tensor(name, shape, dt))

        nsem = [0]

        def sem(name):
            nsem[0] += 1
            return c.enter_context(nc.semaphore(name))

        con = sb("con", [P, C_W])
        ident, tri, ones = con[:, C_ID:C_ID + P], con[:, C_TRI:C_TRI + P], con[:, C_ONE:C_ONE + P]
        causal, rope_p = con[:, C_CAUS:C_CAUS + P], con[:, C_ROPE:C_ROPE + P]
        h = sb("h", [P, T, D])
        hT = sb("hT", [P, K, S])
        ring = [sb(f"ring{i}", [P, UW]) for i in range(UNITS)]
        work = sb("work", [P, 18432])
        small = sb("small", [P, 512])
        zeros = sb("zeros", [P, 256])
        idx = sb("idx", [P, 2 * T], u32)
        top8 = sb("top8", [P, 2 * T, 8], u32)
        ovi = sb("ovi", [P, 32], u32)
        bank = [c.enter_context(nc.psum_tensor(f"bank{i}", [P, 512], f32)) for i in range(8)]
        lnp = work[:, 16384:18432]

        def wk(lo, n, parts=(0, P)):
            return work[parts[0]:parts[1], lo:lo + n]

        def sm(lo, n, parts=(0, P)):
            return small[parts[0]:parts[1], lo:lo + n]

        unit_loaded = [sem(f"unit_loaded{i}") for i in range(UNITS)]
        units_used = sem("units_used")
        const_loaded, x_loaded = sem("const_loaded"), [sem(f"x_loaded{i}") for i in range(T)]
        half_unit = sem("half_unit")
        tile_done = sem("tile_done")
        out_ready, out_done = sem("out_ready"), sem("out_done")
        rows_zeroed, zero_ready = sem("rows_zeroed"), sem("zero_ready")
        dve_step, act_step, pool_step = sem("dve_step"), sem("act_step"), sem("pool_step")

        tiles_written, tiles_turned, tiles_copied = sem("tiles_written"), sem("tiles_turned"), sem("tiles_copied")

        class Turn:

            def __init__(self, src0, copied0, src_all, copied_all):
                self.src0, self.copied0, self.src_all, self.copied_all = src0, copied0, src_all, copied_all

        turns, written, copied = {}, 0, 0
        for name in ("x", "o1", "mix0", "ffn0", "mix1", "rms0", "att2", "rms1"):
            chunks = 4 if name == "att2" else K
            src0, copied0 = written, copied
            written += T if name != "x" else 0
            copied += T * chunks // 4
            turns[name] = Turn(src0, copied0, written, copied)

        class Parameters:

            def __init__(self):
                self.rope, self.subg, self.lam = sem("par_rope"), sem("par_subg"), sem("par_lam")
                self.ln0, self.ln1, self.ln2 = sem("par_ln0"), sem("par_ln1"), sem("par_ln2")
                self.ln3, self.pscale, self.rms0 = sem("par_ln3"), sem("par_pscale"), sem("par_rms0")
                self.conv, self.wab, self.wf = sem("par_conv"), sem("par_wab"), sem("par_wf")
                self.rms1, self.rms2, self.bf = sem("par_rms1"), sem("par_rms2"), sem("par_bf")

        class Steps:

            def __init__(self, name, buffers, used, base, first_row):
                self.xt, self.xT, self.sg = sem(f"{name}_xt"), sem(f"{name}_xT"), sem(f"{name}_sg")
                self.hg, self.ht, self.hT = sem(f"{name}_hg"), sem(f"{name}_ht"), sem(f"{name}_hT")
                self.ysb = sem(f"{name}_ysb")
                self.x_loaded = [sem(f"{name}_x_loaded{i}") for i in range(buffers)]
                self.y_stored = [sem(f"{name}_y_stored{i}") for i in range(buffers)]
                self.used, self.base, self.first_row = used, base, first_row
                self.at_mixture(0)

            def at_mixture(self, l):
                self.n0, self.x0 = E * l, (E + 1) * l
                self.load0 = [16 * (E // 2 + 1) * l, 16 * (E // 2) * l]
                self.store0 = [32 * (E // 2) * l] * 2

        class Routing:

            def __init__(self):
                self.router_loaded, self.logits, self.exp_in = sem("moe_router_loaded"), sem("moe_logits"), sem("moe_exp_in")
                self.exp_out, self.onehots, self.ranks = sem("moe_exp_out"), sem("moe_onehots"), sem("moe_ranks")
                self.indices, self.scattered, self.gathered0 = sem("moe_indices"), sem("moe_scattered"), sem("moe_gathered0")
                self.gathered1, self.summed = sem("moe_gathered1"), sem("moe_summed")

        class Mixture:
            def __init__(self, l):
                self.l, self.F, self.base = l, FDIM[l], first[f"moe{l}"]
                self.upb = 6 if self.F == 512 else 3
                self.ov_units = sem(f"ov{l}_units")
                self.ov = Steps(f"ov{l}", 1, sem(f"ov{l}_used"), 1, E)

            def main(self):
                steps.base = self.base
                steps.at_mixture(self.l)
                return steps

        routing = Routing()
        steps = Steps("main", 2, units_used, 0, 0)
        moe = [Mixture(l) for l in range(3)]

        class Attention:

            def __init__(self):
                self.v, self.raw, self.perm = sem("at_v"), sem("at_raw"), sem("at_perm")
                self.rope, self.sc, self.negmax = sem("at_rope"), sem("at_sc"), sem("at_negmax")
                self.exp, self.a, self.at = sem("at_exp"), sem("at_a"), sem("at_at")
                self.aT, self.av, self.o = sem("at_aT"), sem("at_av"), sem("at_o")
                self.lam_in, self.lam_ex, self.var = sem("at_lam_in"), sem("at_lam_ex"), sem("at_var")
                self.std, self.cqp, self.cq = sem("at_std"), sem("at_cqp"), sem("at_cq")
                self.ckp, self.ck = sem("at_ckp"), sem("at_ck")

        class Pooling:

            def __init__(self):
                self.u, self.p, self.g = sem("po_u"), sem("po_p"), sem("po_g")
                self.y = sem("po_y")

        class Second:

            def __init__(self):
                self.copied, self.conv, self.pairs = sem("b2_copied"), sem("b2_conv"), sem("b2_pairs")
                self.sp_in, self.sp_e, self.decay = sem("b2_sp_in"), sem("b2_sp_e"), sem("b2_decay")
                self.tau, self.m2, self.mult = sem("b2_tau"), sem("b2_m2"), sem("b2_mult")
                self.free, self.f, self.f_in = sem("b2_free"), sem("b2_f"), sem("b2_f_in")
                self.f_e, self.c, self.lruT = sem("b2_f_e"), sem("b2_c"), sem("b2_lruT")

        par, at, po, b2 = Parameters(), Attention(), Pooling(), Second()
        ln3_done = sem("ln3_done")
        norm_var, norm_std = sem("norm_var"), sem("norm_std")

        def waits(eng, step_sem):
            count = [0]

            def link(ins):
                count[0] += 1
                ins.then_inc(step_sem, 1)
                eng.wait_ge(step_sem, count[0])
            return link

        def wait_unit(eng, u):
            eng.wait_ge(unit_loaded[u % UNITS], 16 * (u // UNITS + 1))

        t_units = [u for n in ("qk", "pin", "rec", "gate", "q2", "k2")
                   for u in range(first[n], first[n] + {"qk": 8, "pin": 4}.get(n, 2))]
        b_halves = [first[n] + 2 * i for n, k in (("v", 2), ("wo", 2), ("pout", 2), ("v2", 1), ("out2", 2))
                    for i in range(k)]

        def wait_half(eng, u, half):
            if half:
                eng.wait_ge(units_used, u + 1)
            else:
                eng.wait_ge(half_unit, t_units.index(u) + 1)

        def wait_tile(eng, u, tt):
            if tt == T - 1:
                eng.wait_ge(units_used, u + 2)
            else:
                eng.wait_ge(tile_done, 3 * b_halves.index(u) + tt + 1)

        def over_blocks(eng, m, body):
            n = UNITS // m.upb
            for s in range(n):
                body(0, s, n)
            with eng.Fori(1, E // n) as i:
                for s in range(n):
                    body(i, s, n)

        xg = [wk(1024 * i, 1024, (0, BLK)) for i in range(2)]
        xgT = [wk(2048 + 512 * i, 512) for i in range(2)]
        sg, hg = wk(3072, 512, (BLK, P)), wk(3584, 512, (BLK, P))
        hgT = wk(4096, 256)
        ysb = [wk(4352 + 512 * i, 512) for i in range(2)]
        wr = wk(5376, 288).rearrange("p (k n) -> p k n", k=K)
        rbias = wk(5664, 36)
        logit = wk(5700, 144).rearrange("p (t n) -> p t n", t=T)
        gpad = wk(5844, 32).rearrange("p (t n) -> p t n", t=T)
        g8 = wk(5876, 32).rearrange("p (t n) -> p t n", t=T)
        e8 = wk(5908, 32).rearrange("p (t n) -> p t n", t=T)
        emask = wk(5940, 128).rearrange("p (t n) -> p t n", t=T)
        em = wk(6068, 128).rearrange("p (t n) -> p t n", t=T)
        hot1 = wk(6196, 128).rearrange("p (t n) -> p t n", t=T)
        hot2 = wk(6324, 128).rearrange("p (t n) -> p t n", t=T)
        hots = wk(6452, 128).rearrange("p (t n) -> p t n", t=T)
        rank = wk(6580, 128).rearrange("p (t n) -> p t n", t=T)
        rowE = wk(6708, 128).rearrange("p (t n) -> p t n", t=T)
        nblk, ovend, ovdiff, zero32 = (wk(6836 + 32 * i, 32) for i in range(4))
        ovcmp = wk(6964, 512).rearrange("p (j n) -> p j n", j=16)
        ovf = wk(7476, 17)
        tokf = wk(7500, 64)
        wts = wk(7564, 8).rearrange("p (k t) -> p k t", k=2)
        ygat = [[wk(8192 + 2048 * i + 1024 * k, 1024) for k in range(2)] for i in range(2)]
        hn = wk(12288, 4096).rearrange("p (t d) -> p t d", t=T)
        GU, DN, XT, HT, RT, CT = bank[0], bank[1], bank[2], bank[3], bank[4], bank[5]

        v1 = wk(0, 4096).rearrange("p (t d) -> p t d", t=T)
        o1 = wk(4096, 4096).rearrange("p (t d) -> p t d", t=T)
        qT = [wk(8192 + 512 * i, 512) for i in range(4)]
        kT = [wk(10240 + 512 * i, 512) for i in range(4)]
        prob = [wk(12288 + 512 * i, 512) for i in range(2)]
        abuf = [wk(13312 + 512 * i, 512) for i in range(2)]
        aT = wk(14336, 512)
        raw = [wk(14848 + 512 * i, 512) for i in range(2)]
        rtmp = wk(15872, 512)
        ropec, ropes = wk(16384, 512), wk(16896, 512)
        subg = sm(0, 128)
        lamv = sm(128, 256).rearrange("p (a n) -> p a n", a=4)
        stats = sm(384, 12).rearrange("p (a n) -> p a n", a=2)
        mv = sm(396, 8).rearrange("p (t n) -> p t n", t=T)
        rstd = sm(404, 4)
        mx, negmax = sm(408, 2), sm(410, 2)
        rs, rr = sm(412, 2), sm(414, 2)
        lam = sm(416, 4)
        sumsq = sm(420, 32).rearrange("p (t n) -> p t n", t=T)
        orstd = sm(452, 32).rearrange("p (t n) -> p t n", t=T)
        ojunk = sb("ojunk", [P, P])[:, :]

        PAD = 16
        uT = wk(0, K * (S + PAD)).rearrange("p (k n) -> p k n", k=K)
        win = [wk(4224 + 1056 * i, 1056).rearrange("p (k n) -> p k n", k=2) for i in range(2)]
        pT = wk(6336, 4096).rearrange("p (k n) -> p k n", k=K)
        yT = wk(10432, 4096).rearrange("p (k n) -> p k n", k=K)
        pscale = sm(0, 8)

        def quad(lo):
            return wk(lo, 2048).rearrange("p (k n) -> p k n", k=4)

        bx, br, bi, bg, be = (quad(2048 * i) for i in range(5))
        q2T, k2T, v2 = quad(10240), quad(12288), quad(14336)
        fb = [wk(lo, 512, (0, 8)) for lo in (16384, 16896, 17920, 14336)]
        lg2, p2T, nck = [wk(0 + 512 * i, 512) for i in range(2)], wk(1024, 512), [wk(1536 + 512 * i, 512) for i in range(2)]
        att2 = wk(4096, 2048).rearrange("p (t d) -> p t d", t=T)
        p2 = [wk(2560 + 512 * i, 512) for i in range(2)]
        wab = wk(17408, 512).rearrange("p (a c n) -> p a c n", a=2, c=4)
        convp = sm(0, 32)
        wf = sm(32, 64).rearrange("p (k n) -> p k n", k=K)
        bfg = sm(96, 1, (0, 8))
        spl = sm(100, 20)
        cq = sm(128, 32).rearrange("p (t n) -> p t n", t=T)
        rs2, rr2 = sm(160, 4), sm(164, 4)
        taps = convp[:, 0:16].rearrange("p (w c) -> p w c", w=4)
        SERIES = 8
        R_REC, R_GATE, R_F, R_Q, R_LRU, R_K, R_V, R_END = 0, 4, 8, 9, 13, 21, 25, 29

        block = c.enter_context(nc.Block())

        @block.sync
        def _(sp):
            def load(u):
                if u >= UNITS:
                    sp.wait_ge(units_used, u - UNITS + 1)
                sp.dma_start(ring[u % UNITS][:, :], units[u]).then_inc(unit_loaded[u % UNITS], 16)

            def expert_units(m, l, e):
                gate, up, down = experts[l]
                if m.F == 512:
                    for kk in range(2):
                        for a in (gate, up):
                            yield a[e, 512 * kk:512 * kk + 512, :].rearrange("(k p) n -> p k n", p=P)
                    for kk in range(2):
                        yield down[e, 256 * kk:256 * kk + 256, :].rearrange("(k p) n -> p k n", p=P)
                else:
                    for a in (gate, up):
                        yield a[e].rearrange("(k p) n -> p k n", p=P)
                    yield down[e].rearrange("(k p) n -> p k n", p=P)

            def mixture(l):
                m = moe[l]
                main = m.main()
                n = UNITS // m.upb

                def expert(i, s):
                    for q, src in enumerate(expert_units(m, l, n * i + s)):
                        u = m.base + m.upb * s + q
                        sp.wait_ge(units_used, u - UNITS + 1 + UNITS * i)
                        sp.dma_start(ring[u % UNITS][:, :], src).then_inc(unit_loaded[u % UNITS], 16)

                def rows_of(b, s, block_index):
                    sp.dma_start(xg[s], x_rows[bass.ts(block_index, BLK), :]).then_inc(b.x_loaded[s], 16)

                for s in range(n):
                    expert(0, s)
                sp.wait_ge(routing.scattered, 16 * 2 * T * (l + 1))
                for s in range(n):
                    if s >= 2:
                        sp.wait_ge(main.xt, main.x0 + s - 1)
                    rows_of(main, s % 2, s)
                with sp.Fori(1, E // n) as i:
                    for s in range(n):
                        sp.wait_ge(main.xt, main.x0 + n * i + s - 1)
                        rows_of(main, s % 2, n * i + s)
                        expert(i, s)
                sp.wait_ge(main.xt, main.x0 + E - 1)
                rows_of(main, 0, E)
                sp.wait_ge(routing.indices, m.l + 1)
                count = sp.value_load(ovi[0:1, 16:17], min_val=0, max_val=OVF)
                with sp.If(count > 0):
                    sp.wait_ge(units_used, m.base + E * m.upb)
                    sp.wait_ge(main.xt, main.x0 + E + 1)
                    sp.sem_inc(m.ov.used, 1)
                    with sp.Fori(0, count) as j:
                        e = sp.value_load(ovi[0:1, bass.ds(j, 1)], min_val=0, max_val=E - 1)
                        sp.wait_ge(m.ov.used, m.upb * j + 1)
                        rows_of(m.ov, 0, E + j)
                        for q, src in enumerate(expert_units(m, l, e)):
                            u = m.base + q
                            sp.dma_start(ring[u % UNITS][:, :], src).then_inc(m.ov_units, 16)

            sp.dma_start(con[:, :], t["con"]).then_inc(const_loaded, 16)
            for i in range(T):
                sp.dma_start(h[:, i, :], t["x"][0, P * i:P * i + P, :]).then_inc(x_loaded[i], 16)
            sp.dma_start(work[:, 16384:17408], t["rope"]).then_inc(par.rope, 16)
            for u in range(UNITS):
                load(u)
            sp.wait_ge(zero_ready, 1)
            sp.dma_start(x_rows.rearrange("(p n) (q c) -> p (n q) c", p=P, c=256),
                         zeros[:, :].unsqueeze(1).to_broadcast([P, rows_ // P * 4, 256])).then_inc(rows_zeroed, 16)
            sp.dma_start(y_rows[E * BLK:rows_].rearrange("(p n) (q c) -> p (n q) c", p=P, c=256),
                         zeros[:, :].unsqueeze(1).to_broadcast([P, (rows_ - E * BLK) // P * 4, 256]))\
                .then_inc(rows_zeroed, 16)
            for u in range(UNITS, first["moe0"]):
                load(u)
            mixture(0)
            for u in range(first["pin"], first["moe1"]):
                load(u)
            mixture(1)
            for u in range(first["rec"], first["moe2"]):
                load(u)
            mixture(2)

            for tt in range(T):
                sp.wait_ge(out_ready, tt + 1)
                sp.dma_start(t["out"][0, P * tt:P * tt + P, :], hn[:, tt, :]).then_inc(out_done, 16)
            sp.wait_ge(out_done, 16 * T)

        @block.tensor
        def _(pe):
            def project_t(u, banks, half, ks=range(K)):
                v = ring[u % UNITS][:, :].rearrange("p (k n) -> p k n", k=K)
                for k in ks:
                    mm = pe.matmul(banks[:, :], v[:, k, 128 * half:128 * half + 128], hT[:, k, :],
                                   start=(k == 0), stop=(k == K - 1))
                    if k == K - 1:
                        mm.then_inc(units_used if half else half_unit, 1)

            def project_b(u, operand, banks):
                for kk in range(2):
                    wait_unit(pe, u + kk)
                    v = ring[(u + kk) % UNITS][:, :].rearrange("p (k n) -> p k n", k=4)
                    for tt in range(T):
                        for k in range(4):
                            mm = pe.matmul(banks[tt][:, :], operand[:, 4 * kk + k, P * tt:P * tt + P], v[:, k, :],
                                           start=(kk + k == 0), stop=(kk + k == 4))
                        if tt == T - 1:
                            mm.then_inc(units_used, 1)
                        elif kk == 1:
                            mm.then_inc(tile_done, 1)

            def turn(name, src, chunks=K):
                s = turns[name]
                for tt in range(T):
                    if name == "x":
                        pe.wait_ge(x_loaded[tt], 16)
                    else:
                        pe.wait_ge(tiles_written, s.src0 + tt + 1)
                    for kk in range(chunks // 4):
                        for k in range(4):
                            mm = pe.transpose(bank[(2 * tt + kk) % 8][:, P * k:P * k + P],
                                              src[:, tt, P * (4 * kk + k):P * (4 * kk + k) + P], ident)
                        mm.then_inc(tiles_turned, 1)

            pe.wait_ge(const_loaded, 16)
            turn("x", h)
            pe.wait_ge(tiles_copied, turns["x"].copied_all)
            for n in range(2):
                project_b(first["v"] + 2 * n, hT, bank[4 * n:4 * n + 4])

            def chunk_unit(cc):
                pair, n = cc // 4, cc % 4
                return first["qk"] + 2 * pair + n // 2, n % 2

            def head_place(hh):
                return qT[hh % 4], kT[hh % 4]

            def scores(g):
                hh, qb = g // 4, g % 4
                if qb == 0:
                    pe.wait_ge(at.rope, 4 * (hh // 2) + 3 + hh % 2)
                q_, k_ = head_place(hh)
                for m in range(2):
                    rows = slice(64 * m, 64 * m + 64)
                    pe.matmul(bank[2 + 2 * (g % 2) + m][:, 0:P * (qb + 1)], q_[rows, P * qb:P * qb + P],
                              k_[rows, 0:P * (qb + 1)], start=True, stop=True).then_inc(at.sc, 1)

            def values(g):
                hh, qb = g // 4, g % 4
                pe.wait_ge(at.a, g + 1)
                for b in range(qb + 1):
                    mm = pe.transpose(bank[6][:, P * b:P * b + P], abuf[g % 2][:, P * b:P * b + P], ident)
                mm.then_inc(at.at, 1)
                pe.wait_ge(at.aT, g + 1)
                for b in range(qb + 1):
                    mm = pe.matmul(bank[7][:, 0:P], aT[:, P * b:P * b + P], v1[:, b, P * hh:P * hh + P],
                                   start=(b == 0), stop=(b == qb))
                mm.then_inc(at.av, 1)

            def permute(cc):
                pe.wait_ge(at.raw, cc + 1)
                pe.matmul(bank[cc % 2][:, :], rope_p, raw[cc % 2], start=True, stop=True).then_inc(at.perm, 1)

            pe.wait_ge(at.v, 2 * T)
            for step in range(5 * 8):
                pair, st = step // 8, step % 8
                if pair < 4:
                    cc = 4 * pair + st // 2
                    u, half = chunk_unit(cc)
                    if st % 2 == 0:
                        if cc >= 2:
                            pe.wait_ge(at.rope, cc - 1)
                        wait_unit(pe, u)
                    project_t(u, bank[cc % 2], half, range(4 * (st % 2), 4 * (st % 2) + 4))
                if pair >= 1:
                    scores(step - 8)
                if st % 2 == 0 and 1 <= 4 * pair + st // 2 <= 16:
                    permute(4 * pair + st // 2 - 1)
                if step > 8:
                    values(step - 9)
            values(31)
            turn("o1", o1)
            pe.wait_ge(tiles_copied, turns["o1"].copied_all)
            for n in range(2):
                project_b(first["wo"] + 2 * n, hT, bank[4 * n:4 * n + 4])
            turn("mix0", h)

            def mixture(l, before):
                m = moe[l]
                main = m.main()
                F, half_f = m.F, m.F // 128
                pe.wait_ge(tiles_copied, turns[before].copied_all)
                pe.wait_ge(routing.router_loaded, 64 * l + (64 if l < 2 else 112))
                for tt in range(T):
                    for k in range(K):
                        mm = pe.matmul(RT[:, 36 * tt:36 * tt + 36], hT[:, k, P * tt:P * tt + P], wr[:, k, :],
                                       start=(k == 0), stop=(k == K - 1))
                mm.then_inc(routing.logits, 1)
                pe.wait_ge(routing.onehots, l + 1)
                for tt in range(T):
                    for t0 in range(tt + 1):
                        mm = pe.matmul(CT[:, 32 * tt:32 * tt + 32], tri if t0 == tt else ones, hots[:, t0, :],
                                       start=(t0 == 0), stop=(t0 == tt))
                for t0 in range(T):
                    mm = pe.matmul(CT[:, 128:160], ones, hots[:, t0, :], start=(t0 == 0), stop=(t0 == T - 1))
                mm.then_inc(routing.ranks, 1)

                def turn_block(k, out, rows, eye):
                    if k == 0:
                        return pe.matmul(out, rows, eye, start=True, stop=True)
                    return pe.transpose(out, rows, eye)

                def turn_rows(b, s, loaded):
                    pe.wait_ge(b.x_loaded[s], b.load0[s] + loaded)
                    for k in range(K):
                        mm = turn_block(k, XT[:, BLK * k:BLK * k + BLK], xg[s][:, P * k:P * k + P],
                                        ident[0:BLK, 0:BLK])
                    mm.then_inc(b.xt, 1)

                def expert(b, j, s, unit, need, ahead):
                    xT_ = xgT[s].rearrange("p (k n) -> p k n", k=K)
                    pe.wait_ge(b.xT, b.x0 + j + 1)
                    if F == 512:
                        for kk in range(2):
                            need(2 * kk)
                            need(2 * kk + 1)
                            for k in range(4):
                                for a in range(2):
                                    v = unit(2 * kk + a).rearrange("p (k n) -> p k n", k=4)
                                    mm = pe.matmul(GU[BLK * a:BLK * a + BLK, :], xT_[:, 4 * kk + k, :], v[:, k, :],
                                                   start=(kk + k == 0), stop=(kk + k == 4))
                            mm.then_inc(b.used, 2)
                    else:
                        need(0)
                        need(1)
                        for k in range(K):
                            for a in range(2):
                                v = unit(a).rearrange("p (k n) -> p k n", k=K)
                                mm = pe.matmul(GU[BLK * a:BLK * a + BLK, 0:F], xT_[:, k, :], v[:, k, :],
                                               start=(k == 0), stop=(k == K - 1))
                        mm.then_inc(b.used, 2)
                    if ahead is not None:
                        ahead()
                    pe.wait_ge(b.hg, b.n0 + j + 1)
                    for k in range(half_f):
                        mm = turn_block(k, HT[:, BLK * k:BLK * k + BLK], hg[:, P * k:P * k + P], ident[BLK:P, BLK:P])
                    mm.then_inc(b.ht, 1)
                    pe.wait_ge(b.hT, b.n0 + j + 1)
                    hT_ = hgT.rearrange("p (k n) -> p k n", k=4)
                    for kk in range(F // 256):
                        need(m.upb - F // 256 + kk)
                        v = unit(m.upb - F // 256 + kk).rearrange("p (k n) -> p k n", k=2)
                        for k in range(2):
                            for n in range(2):
                                mm = pe.matmul(DN[BLK * n:BLK * n + BLK, :], hT_[:, 2 * kk + k, :],
                                               v[:, k, 512 * n:512 * n + 512],
                                               start=(kk + k == 0), stop=(2 * kk + k == half_f - 1))
                        mm.then_inc(b.used, 1)

                turn_rows(main, 0, 16)

                def body(i, s, n):
                    def unit(q):
                        return ring[(m.base + m.upb * s + q) % UNITS][:, :]

                    def need(q):
                        u = m.base + m.upb * s + q
                        pe.wait_ge(unit_loaded[u % UNITS], 16 * (u // UNITS + 1) + 16 * i)

                    def ahead():
                        nb = s + 1
                        turn_rows(main, nb % 2, 16 * (nb // 2 + 1) + 8 * n * i)
                    expert(main, n * i + s, s % 2, unit, need, ahead)
                over_blocks(pe, m, body)

                pe.wait_ge(routing.indices, m.l + 1)
                count = pe.value_load(ovi[0:1, 16:17], min_val=0, max_val=OVF)
                with pe.If(count > 0):
                    with pe.Fori(0, count) as j:
                        turn_rows(m.ov, 0, 16 * j + 16)
                        expert(m.ov, j, 0, lambda q: ring[(m.base + q) % UNITS][:, :],
                               lambda q: pe.wait_ge(m.ov_units, 16 * m.upb * j + 16 * m.upb), None)

            mixture(0, "mix0")
            turn("ffn0", h)
            pe.wait_ge(tiles_copied, turns["ffn0"].copied_all)
            for u in range(4):
                wait_unit(pe, first["pin"] + u)
                for half in range(2):
                    project_t(first["pin"] + u, bank[2 * u + half], half)
            u = first["pgrp"]
            wait_unit(pe, u)
            v = ring[u % UNITS][:, :].rearrange("p (k n) -> p k n", k=K)
            for g in range(4):
                pe.wait_ge(po.p, g + 1)
                for half in range(2):
                    for k in range(2):
                        mm = pe.matmul(bank[2 * g + half][:, :], v[:, 2 * g + k, P * half:P * half + P],
                                       pT[:, 2 * g + k, :], start=(k == 0), stop=(k == 1))
                    if g < 3 or half == 0:
                        mm.then_inc(po.g, 1)
            mm.then_inc(units_used, 1)
            pe.wait_ge(po.y, K)
            for n in range(2):
                project_b(first["pout"] + 2 * n, yT, bank[4 * n:4 * n + 4])
            turn("mix1", h)
            mixture(1, "mix1")
            turn("rms0", hn)
            def bank_of(r):
                if r >= 8:
                    pe.wait_ge(b2.copied, r - 7)
                return bank[r % 8]

            def results(name, r):
                for u in range(first[name], first[name] + 2):
                    wait_unit(pe, u)
                    for half in range(2):
                        project_t(u, bank_of(r), half)
                        r += 1

            pe.wait_ge(tiles_copied, turns["rms0"].copied_all)
            results("rec", R_REC)
            results("gate", R_GATE)
            pe.wait_ge(par.wf, 16)
            bk = bank_of(R_F)
            for k in range(K):
                mm = pe.matmul(bk[0:8, :], wf[:, k, :], hT[:, k, :], start=(k == 0), stop=(k == K - 1))
            mm.then_inc(b2.f, 1)
            results("q2", R_Q)
            pe.wait_ge(par.wab, 64)
            for ch in range(4):
                pe.wait_ge(b2.conv, ch + 1)
                for a in range(2):
                    bk = bank_of(R_LRU + 2 * ch + a)
                    for b in range(2):
                        half = slice(64 * b, 64 * b + 64)
                        mm = pe.matmul(bk[half, :], wab[half, a, ch, :], bx[half, ch, :], start=True, stop=True)
                    mm.then_inc(b2.pairs, 1)
            results("k2", R_K)
            pe.wait_ge(b2.copied, R_V - 8 + 4)
            project_b(first["v2"], hT, [bank[(R_V + tt) % 8] for tt in range(T)])
            pe.wait_ge(b2.copied, R_END)
            pe.wait_ge(b2.c, 1)
            for tt in range(T):
                mm = pe.transpose(bank[7][:, 8 * tt:8 * tt + 8], fb[0][:, P * tt:P * tt + P], ident[0:8, 0:8])
            mm.then_inc(at.cqp, 1)
            pe.wait_ge(at.cq, 1)

            def spread_c(hh):
                if hh >= 2:
                    pe.wait_ge(at.ck, hh - 1)
                pe.matmul(bank[6 + hh % 2][:, :], ident[0:8, hh:hh + 1].to_broadcast([8, P]), fb[0],
                          start=True, stop=True).then_inc(at.ckp, 1)

            def scores2(g):
                hh, qb = g // 4, g % 4
                half = slice(64 * (hh % 2), 64 * (hh % 2) + 64)
                pe.matmul(bank[g % 2][:, 0:P * (qb + 1)], q2T[half, hh // 2, P * qb:P * qb + P],
                          k2T[half, hh // 2, 0:P * (qb + 1)], start=True, stop=True).then_inc(at.sc, 1)

            def values2(g):
                hh, qb = g // 4, g % 4
                pe.wait_ge(at.exp, 64 + g + 1)
                for b in range(qb + 1):
                    mm = pe.transpose(bank[2 + g % 2][:, P * b:P * b + P], p2[g % 2][:, P * b:P * b + P], ident)
                mm.then_inc(at.at, 1)
                if g >= 2:
                    pe.wait_ge(at.o, 32 + g - 1)
                pe.wait_ge(at.aT, 32 + g + 1)
                for b in range(qb + 1):
                    mm = pe.matmul(bank[4 + g % 2][:, 0:64], p2T[:, P * b:P * b + P], v2[:, b, 64 * hh:64 * hh + 64],
                                   start=(b == 0), stop=(b == qb))
                mm.then_inc(at.av, 1)

            spread_c(0)
            scores2(0)
            for g in range(32):
                if g < 31:
                    scores2(g + 1)
                if g % 4 == 1 and g < 28:
                    spread_c(g // 4 + 1)
                values2(g)
            turn("att2", att2, 4)
            pe.wait_ge(tiles_copied, turns["att2"].copied_all)
            pe.wait_ge(b2.lruT, 4)
            for n in range(2):
                project_b(first["out2"] + 2 * n, hT, bank[4 * n:4 * n + 4])
            turn("rms1", hn)
            mixture(2, "rms1")

        @block.scalar
        def _(act):
            def turned(name, chunks=K):
                s = turns[name]
                for tt in range(T):
                    for kk in range(chunks // 4):
                        n = chunks // 4 * tt + kk + 1
                        act.wait_ge(tiles_turned, s.copied0 + n)
                        act.activation(hT[:, 4 * kk:4 * kk + 4, P * tt:P * tt + P],
                                       bank[(2 * tt + kk) % 8][:, :].rearrange("p (k n) -> p k n", k=4),
                                       ACT.Copy).then_inc(tiles_copied, 1)

            norms = [0]

            def norm_root():
                norms[0] += 1
                act.wait_ge(norm_var, norms[0])
                act.activation(rstd, rstd, ACT.Sqrt).then_inc(norm_std, 1)

            act.wait_ge(at.lam_in, 1)
            act.activation(lam[:, 0:2], lam[:, 0:2], ACT.Exp).then_inc(at.lam_ex, 1)
            turned("x")
            for n in range(2):
                for tt in range(T):
                    wait_tile(act, first["v"] + 2 * n, tt)
                    act.activation(v1[:, tt, 512 * n:512 * n + 512], bank[4 * n + tt][:, :], ACT.Copy)\
                       .then_inc(at.v, 1)

            def copy_turned(g):
                act.wait_ge(at.at, g + 1)
                act.activation(aT[:, 0:P * (g % 4 + 1)], bank[6][:, 0:P * (g % 4 + 1)], ACT.Copy).then_inc(at.aT, 1)

            def copy_out(g):
                hh, qb = g // 4, g % 4
                act.wait_ge(at.av, g + 1)
                act.activation(o1[:, qb, P * hh:P * hh + P], bank[7][:, 0:P], ACT.Copy)
                act.activation(ojunk, bank[7][:, 0:P], ACT.Square, accum_out=sumsq[:, qb, hh:hh + 1])\
                   .then_inc(at.o, 1)

            for step in range(5 * 8 + 1):
                if step > 8:
                    copy_turned(step - 9)
                if 8 <= step < 40:
                    g = step - 8
                    for m in range(2):
                        act.wait_ge(at.negmax, 2 * g + m + 1)
                        n = P * (g % 4 + 1)
                        act.activation(prob[m][:, 0:n], bank[2 + 2 * (g % 2) + m][:, 0:n], ACT.Exp,
                                       bias=negmax[:, m:m + 1], scale=0.125, accum_out=rs[:, m:m + 1])\
                           .then_inc(at.exp, 1)
                if step > 8:
                    copy_out(step - 9)
                if step < 32 and step % 2:
                    cc = step // 2
                    pair, n = cc // 4, cc % 4
                    wait_half(act, first["qk"] + 2 * pair + n // 2, n % 2)
                    act.activation(raw[cc % 2], bank[cc % 2][:, :], ACT.Copy).then_inc(at.raw, 1)
            act.wait_ge(at.var, 1)
            act.activation(orstd, orstd, ACT.Sqrt).then_inc(at.std, 1)
            turned("o1")
            norm_root()
            turned("mix0")

            def mixture(l):
                m = moe[l]
                main = m.main()
                F = m.F
                act.wait_ge(routing.exp_in, l + 1)
                act.activation(tokf[:, 20:40], tokf[:, 0:20], ACT.Exp).then_inc(routing.exp_out, 1)

                def expert(b, j, s, reuse):
                    act.wait_ge(b.used, b.base + m.upb * j + m.upb - F // 256)
                    act.activation(sg[:, 0:F], GU[0:BLK, 0:F], ACT.Silu).then_inc(b.sg, 1)
                    act.wait_ge(b.used, b.base + m.upb * j + m.upb)
                    if reuse is not None:
                        act.wait_ge(b.y_stored[s], b.store0[s] + reuse)
                    act.activation(ysb[s], DN[:, :], ACT.Copy).then_inc(b.ysb, 1)
                    act.wait_ge(b.ysb, b.n0 + j + 1)
                    block_row = j + b.first_row
                    for n in range(2):
                        act.dma_start(y_rows[bass.ts(block_row, BLK), 512 * n:512 * n + 512],
                                      ysb[s][BLK * n:BLK * n + BLK, :]).then_inc(b.y_stored[s], 16)

                def body(i, s, n):
                    once = type(i) is int
                    reuse = None if once and s < 2 and l == 0 else 32 * (s // 2) + 16 * n * i
                    expert(main, n * i + s, s % 2, reuse)
                over_blocks(act, m, body)
                act.wait_ge(routing.indices, m.l + 1)
                count = act.value_load(ovi[0:1, 16:17], min_val=0, max_val=OVF)
                with act.If(count > 0):
                    for s in range(2):
                        act.wait_ge(main.y_stored[s], main.store0[s] + 32 * E // 2)
                    with act.Fori(0, count) as j:
                        expert(m.ov, j, 0, None)
                        act.wait_ge(m.ov.y_stored[0], 32 * j + 32)

            mixture(0)
            norm_root()
            turned("ffn0")
            for r in range(K):
                wait_half(act, first["pin"] + r // 2, r % 2)
                act.activation(uT[:, r, PAD:PAD + S], bank[r][:, :], ACT.Copy).then_inc(po.u, 1)
            act.wait_ge(par.pscale, 16)
            for r in range(K):
                if r < K - 1:
                    act.wait_ge(po.g, r + 1)
                else:
                    act.wait_ge(units_used, first["pgrp"] + 1)
                act.activation(yT[:, r, :], bank[r][:, :], ACT.Copy, scale=pscale[:, r:r + 1]).then_inc(po.y, 1)
            norm_root()
            turned("mix1")
            mixture(1)
            norm_root()
            norm_root()
            turned("rms0")
            def copy_result(dst, r, func=ACT.Copy, rows=P, **kw):
                act.activation(dst, bank[r % 8][0:rows, :], func, **kw).then_inc(b2.copied, 1)

            act.wait_ge(b2.sp_in, 1)
            act.activation(spl[:, 0:4], spl[:, 0:4], ACT.Exp).then_inc(b2.sp_e, 1)
            for r in range(4):
                wait_half(act, first["rec"] + r // 2, r % 2)
                copy_result(be[:, r, :], R_REC + r)
            for r in range(4):
                wait_half(act, first["gate"] + r // 2, r % 2)
                copy_result(bg[:, r, :], R_GATE + r, ACT.Gelu_apprx_tanh)
            act.wait_ge(b2.f, 1)
            act.wait_ge(par.bf, 16)
            copy_result(fb[0], R_F, ACT.Identity, 8, bias=bfg)
            for r in range(4):
                wait_half(act, first["q2"] + r // 2, r % 2)
                copy_result(q2T[:, r, :], R_Q + r, scale=0.125)
            act.wait_ge(b2.f_in, 1)
            act.activation(fb[1], fb[1], ACT.Exp).then_inc(b2.f_e, 1)
            for ch in range(4):
                for a in range(2):
                    act.wait_ge(b2.pairs, 2 * ch + a + 1)
                    copy_result((br, bi)[a][:, ch, :], R_LRU + 2 * ch + a, ACT.Sigmoid,
                                bias=convp[:, 20 + 4 * a + ch:21 + 4 * a + ch])
            for ch in range(4):
                act.wait_ge(b2.decay, ch + 1)
                act.activation(be[:, ch, :], br[:, ch, :], ACT.Exp, scale=-1.0).then_inc(b2.free, 1)
            act.wait_ge(b2.free, 4)
            for ch in range(4):
                act.activation(br[:, ch, :], br[:, ch, :], ACT.Tanh).then_inc(b2.tau, 1)
            for r in range(4):
                wait_half(act, first["k2"] + r // 2, r % 2)
                copy_result(k2T[:, r, :], R_K + r)
            for ch in range(4):
                act.wait_ge(b2.m2, ch + 1)
                act.activation(br[:, ch, :], br[:, ch, :], ACT.Sqrt).then_inc(b2.mult, 1)
            act.wait_ge(b2.c, 1)
            for tt in range(T):
                wait_tile(act, first["v2"], tt)
                copy_result(v2[:, tt, :], R_V + tt)
            act.wait_ge(at.cqp, 1)
            act.activation(cq, bank[7][:, 0:32].rearrange("p (t n) -> p t n", t=T), ACT.Copy).then_inc(at.cq, 1)
            act.wait_ge(b2.lruT, 4)

            def copy_c(hh):
                act.wait_ge(at.ckp, hh + 1)
                act.activation(nck[hh % 2], bank[6 + hh % 2][:, :], ACT.Copy, scale=-1.0).then_inc(at.ck, 1)

            def exp2(g):
                n = P * (g % 4 + 1)
                act.wait_ge(at.negmax, 64 + g + 1)
                act.activation(p2[g % 2][:, 0:n], lg2[g % 2][:, 0:n], ACT.Exp, bias=negmax[:, g % 2:g % 2 + 1],
                               accum_out=rs2[:, g % 4:g % 4 + 1]).then_inc(at.exp, 1)

            copy_c(0)
            exp2(0)
            for g in range(32):
                if g < 31:
                    exp2(g + 1)
                n = P * (g % 4 + 1)
                act.wait_ge(at.at, 32 + g + 1)
                act.activation(p2T[:, 0:n], bank[2 + g % 2][:, 0:n], ACT.Copy).then_inc(at.aT, 1)
                if g % 4 == 1 and g < 28:
                    copy_c(g // 4 + 1)
            turned("att2", 4)
            norm_root()
            turned("rms1")
            mixture(2)
            norm_root()

        @block.vector
        def _(dve):
            link = waits(dve, dve_step)
            norms = [0]

            def root():
                norms[0] += 1
                dve.wait_ge(norm_std, norms[0])
                link(dve.reciprocal(rstd, rstd))

            def layer_norm(which, done, count0):
                for tt in range(T):
                    for n in range(2):
                        ins = dve.bn_stats(out=stats[:, n, :], in_=h[:, tt, 512 * n:512 * n + 512])
                        link(ins)
                    link(dve.bn_aggr(out=mv[:, tt, :], in_=stats))
                dve.tensor_scalar(rstd, mv[:, :, 1], 1e-5, None, ALU.add).then_inc(norm_var, 1)
                root()
                dve.wait_ge(which, 32)
                for tt in range(T):
                    link(dve.tensor_scalar(h[:, tt, :], h[:, tt, :], mv[:, tt, 0:1], rstd[:, tt:tt + 1],
                                           ALU.subtract, ALU.mult))
                    link(dve.tensor_tensor(h[:, tt, :], h[:, tt, :], lnp[:, 0:D], ALU.mult))
                    dve.tensor_tensor(h[:, tt, :], h[:, tt, :], lnp[:, D:2 * D], ALU.add).then_inc(done, 1)
                dve.wait_ge(done, count0 + T)

            def rms_norm(gain, par_sem, dst, done, count0, eps):
                for tt in range(T):
                    link(dve.tensor_tensor_reduce(out=dst[:, tt, :], in0=h[:, tt, :], in1=h[:, tt, :], scale=1.0,
                                                  scalar=0.0, op0=ALU.mult, op1=ALU.add,
                                                  accum_out=rstd[:, tt:tt + 1]))
                link(dve.tensor_scalar(rstd, rstd, 1.0 / D, eps, ALU.mult, ALU.add))
                dve.sem_inc(norm_var, 1)
                root()
                dve.wait_ge(par_sem, 16)
                for tt in range(T):
                    dve.scalar_tensor_tensor(out=dst[:, tt, :], in0=h[:, tt, :], scalar=rstd[:, tt:tt + 1], in1=gain,
                                             op0=ALU.mult, op1=ALU.mult).then_inc(done, 1)
                dve.wait_ge(done, count0 + T)

            def residual(u, alpha):
                for n in range(2):
                    for tt in range(T):
                        wait_tile(dve, u + 2 * n, tt)
                        hs = h[:, tt, 512 * n:512 * n + 512]
                        link(dve.scalar_tensor_tensor(out=hs, in0=hs, scalar=alpha, in1=bank[4 * n + tt][:, :],
                                                      op0=ALU.mult, op1=ALU.add))

            dve.memset(zeros[:, :], 0.0).then_inc(zero_ready, 1)
            dve.wait_ge(par.lam, 64)
            for a in range(2):
                link(dve.tensor_tensor(lamv[:, 2 * a, :], lamv[:, 2 * a, :], lamv[:, 2 * a + 1, :], ALU.mult))
                link(dve.tensor_reduce(lam[:, a:a + 1], lamv[:, 2 * a, :], AX, ALU.add))
            dve.sem_inc(at.lam_in, 1)
            dve.wait_ge(at.lam_ex, 1)
            link(dve.tensor_tensor(lam[:, 2:3], lam[:, 1:2], lam[:, 0:1], ALU.subtract))
            link(dve.tensor_scalar(lam[:, 3:4], lam[:, 2:3], -LAMBDA_INIT, None, ALU.add))
            dve.wait_ge(par.subg, 16)
            link(dve.tensor_scalar(subg, subg, 1.0 - LAMBDA_INIT, None, ALU.mult))
            dve.wait_ge(const_loaded, 16)
            dve.wait_ge(par.rope, 16)

            def rope(cc):
                dve.wait_ge(at.perm, cc + 1)
                pair, n = cc // 4, cc % 4
                dst = (qT if n < 2 else kT)[(2 * pair + n % 2) % 4]
                dve.tensor_tensor(rtmp, bank[cc % 2][:, :], ropes, ALU.mult)
                link(dve.tensor_tensor(dst, raw[cc % 2], ropec, ALU.mult))
                dve.tensor_tensor(dst, dst, rtmp, ALU.add).then_inc(at.rope, 1)
                dve.wait_ge(at.rope, cc + 1)

            def maxima(g):
                qb = g % 4
                for m in range(2):
                    dve.wait_ge(at.sc, 2 * g + m + 1)
                    sc = bank[2 + 2 * (g % 2) + m]
                    link(dve.tensor_tensor(sc[:, P * qb:P * qb + P], sc[:, P * qb:P * qb + P], causal, ALU.add))
                    link(dve.tensor_reduce(mx[:, m:m + 1], sc[:, 0:P * (qb + 1)], AX, ALU.max))
                    dve.tensor_scalar(negmax[:, m:m + 1], mx[:, m:m + 1], -0.125, None, ALU.mult).then_inc(at.negmax, 1)

            def combine(g):
                n = P * (g % 4 + 1)
                dve.wait_ge(at.exp, 2 * g + 2)
                link(dve.reciprocal(rr, rs))
                link(dve.tensor_tensor(rr[:, 1:2], rr[:, 1:2], lam[:, 3:4], ALU.mult))
                a = abuf[g % 2][:, 0:n]
                link(dve.tensor_scalar(a, prob[0][:, 0:n], rr[:, 0:1], None, ALU.mult))
                dve.scalar_tensor_tensor(out=a, in0=prob[1][:, 0:n], scalar=rr[:, 1:2], in1=a,
                                         op0=ALU.mult, op1=ALU.add).then_inc(at.a, 1)
                dve.wait_ge(at.a, g + 1)

            for step in range(5 * 8):
                if step >= 8:
                    maxima(step - 8)
                if step % 2 == 0 and 1 <= step // 2 <= 16:
                    rope(step // 2 - 1)
                if step >= 8:
                    combine(step - 8)
            dve.wait_ge(at.o, 32)
            dve.tensor_scalar(orstd, sumsq, 1.0 / P, 1e-5, ALU.mult, ALU.add).then_inc(at.var, 1)
            dve.wait_ge(at.std, 1)
            link(dve.reciprocal(orstd, orstd))
            for tt in range(T):
                for hh in range(8):
                    oo = o1[:, tt, P * hh:P * hh + P]
                    ins = dve.scalar_tensor_tensor(out=oo, in0=oo, scalar=orstd[:, tt, hh:hh + 1], in1=subg,
                                                   op0=ALU.mult, op1=ALU.mult)
                ins.then_inc(tiles_written, 1)
            residual(first["wo"], ALPHA)
            layer_norm(par.ln0, tiles_written, turns["mix0"].src0)

            def mixture(l):
                m = moe[l]
                main = m.main()
                F = m.F
                dve.memset(gpad, -BIG)
                link(dve.memset(zero32, 0.0))
                dve.wait_ge(routing.router_loaded, 64 * l + (64 if l < 2 else 112))
                dve.wait_ge(routing.logits, l + 1)
                for tt in range(T):
                    link(dve.tensor_tensor(logit[:, tt, :], RT[:, 36 * tt:36 * tt + 36], rbias, ALU.add))
                link(dve.tensor_copy(gpad[:, :, 0:NG], logit[:, :, 0:NG]))
                for tt in range(T):
                    link(dve.max(out=g8[:, tt, :], in_=gpad[:, tt, :]))
                    link(dve.max_index(out=top8[:, tt, :], in_max=g8[:, tt, :], in_values=gpad[:, tt, :]))
                link(dve.tensor_copy(tokf[:, 60:64], top8[:, 0:T, 0]))
                for tt in range(T):
                    link(dve.tensor_scalar(emask[:, tt, :], con[:, C_GRP:C_GRP + E], tokf[:, 60 + tt:61 + tt], None,
                                           ALU.is_equal))
                link(dve.tensor_tensor(em, logit[:, :, NG:NG + E], emask, ALU.mult))
                link(dve.tensor_scalar(emask, emask, BIG, -BIG, ALU.mult, ALU.add))
                link(dve.tensor_tensor(em, em, emask, ALU.add))
                for tt in range(T):
                    link(dve.max(out=e8[:, tt, :], in_=em[:, tt, :]))
                    link(dve.max_index(out=top8[:, T + tt, :], in_max=e8[:, tt, :], in_values=em[:, tt, :]))
                link(dve.tensor_copy(tokf[:, 52:56], top8[:, T:2 * T, 0]))
                link(dve.tensor_copy(tokf[:, 56:60], top8[:, T:2 * T, 1]))
                for tt in range(T):
                    link(dve.tensor_scalar(hot1[:, tt, :], con[:, C_IO:C_IO + E], tokf[:, 52 + tt:53 + tt], None,
                                           ALU.is_equal))
                    link(dve.tensor_scalar(hot2[:, tt, :], con[:, C_IO:C_IO + E], tokf[:, 56 + tt:57 + tt], None,
                                           ALU.is_equal))
                dve.tensor_tensor(hots, hot1, hot2, ALU.add).then_inc(routing.onehots, 1)
                for tt in range(T):
                    link(dve.tensor_scalar(tokf[:, 4 * tt:4 * tt + 4], gpad[:, tt, 0:NG], g8[:, tt, 0:1], None,
                                           ALU.subtract))
                link(dve.tensor_tensor(tokf[:, 16:20], e8[:, :, 1], e8[:, :, 0], ALU.subtract))
                dve.sem_inc(routing.exp_in, 1)
                dve.wait_ge(routing.ranks, l + 1)
                link(dve.tensor_copy(rank, CT[:, 0:128].rearrange("p (t n) -> p t n", t=T)))
                link(dve.tensor_copy(ovdiff, CT[:, 128:160]))
                link(dve.memset(nblk, 0.0))
                for lim in rank_thresholds():
                    link(dve.scalar_tensor_tensor(out=nblk, in0=ovdiff, scalar=float(lim), in1=nblk,
                                                  op0=ALU.is_gt, op1=ALU.add))
                link(dve.tensor_tensor_scan(ovend, nblk, zero32, 0.0, ALU.add, ALU.add))
                link(dve.tensor_tensor(ovdiff, ovend, nblk, ALU.subtract))
                link(dve.tensor_scalar(ovdiff, ovdiff, float(BLK), float(E * BLK - MAIN), ALU.mult, ALU.add))
                link(dve.scalar_tensor_tensor(out=ovdiff, in0=con[:, C_IO:C_IO + E], scalar=-float(BLK), in1=ovdiff,
                                              op0=ALU.mult, op1=ALU.add))
                for tt in range(T):
                    link(dve.scalar_tensor_tensor(out=rowE[:, tt, :], in0=rank[:, tt, :], scalar=float(MAIN),
                                                  in1=ovdiff, op0=ALU.is_ge, op1=ALU.mult))
                    link(dve.scalar_tensor_tensor(out=rank[:, tt, :], in0=con[:, C_IO:C_IO + E], scalar=float(BLK),
                                                  in1=rank[:, tt, :], op0=ALU.mult, op1=ALU.add))
                link(dve.tensor_tensor(rowE, rowE, rank, ALU.add))
                link(dve.tensor_tensor(hot1, hot1, rowE, ALU.mult))
                link(dve.tensor_tensor(hot2, hot2, rowE, ALU.mult))
                link(dve.tensor_reduce(tokf[:, 44:48], hot1, AX, ALU.add))
                link(dve.tensor_reduce(tokf[:, 48:52], hot2, AX, ALU.add))
                link(dve.tensor_copy(idx[:, :], tokf[:, 44:52]))
                for j in range(OVF):
                    link(dve.tensor_scalar(ovcmp[:, j, :], ovend, float(j), None, ALU.is_le))
                link(dve.tensor_reduce(ovf[:, 0:OVF], ovcmp[:, 0:OVF, :], AX, ALU.add))
                link(dve.tensor_scalar(ovf[:, 0:OVF], ovf[:, 0:OVF], float(E - 1), None, ALU.min))
                link(dve.tensor_copy(ovf[:, 16:17], ovend[:, E - 1:E]))
                link(dve.tensor_copy(ovi[:, 0:OVF], ovf[:, 0:OVF]))
                dve.tensor_copy(ovi[:, 16:17], ovf[:, 16:17]).then_inc(routing.indices, 1)
                dve.wait_ge(routing.exp_out, l + 1)
                link(dve.tensor_reduce(tokf[:, 40:44], tokf[:, 20:36].rearrange("p (t n) -> p t n", t=T), AX, ALU.add))
                link(dve.tensor_scalar(tokf[:, 16:20], tokf[:, 36:40], 1.0, None, ALU.add))
                link(dve.tensor_tensor(tokf[:, 40:44], tokf[:, 40:44], tokf[:, 16:20], ALU.mult))
                link(dve.reciprocal(wts[:, 0, :], tokf[:, 40:44]))
                link(dve.tensor_tensor(wts[:, 1, :], wts[:, 0, :], tokf[:, 36:40], ALU.mult))

                def copy_rows(b, s, n):
                    dve.wait_ge(b.xt, b.x0 + n)
                    dve.tensor_copy(xgT[s], XT[:, :]).then_inc(b.xT, 1)

                def expert(b, j, s, ahead):
                    dve.wait_ge(b.sg, b.n0 + j + 1)
                    dve.tensor_tensor(hg[:, 0:F], sg[:, 0:F], GU[BLK:P, 0:F], ALU.mult).then_inc(b.hg, 1)
                    if ahead:
                        copy_rows(b, 1 - s, j + 2)
                    dve.wait_ge(b.ht, b.n0 + j + 1)
                    dve.tensor_copy(hgT[:, 0:F // 2], HT[:, 0:F // 2]).then_inc(b.hT, 1)

                copy_rows(main, 0, 1)
                over_blocks(dve, m, lambda i, s, n: expert(main, n * i + s, s % 2, True))
                dve.wait_ge(routing.indices, m.l + 1)
                count = dve.value_load(ovi[0:1, 16:17], min_val=0, max_val=OVF)
                with dve.If(count > 0):
                    with dve.Fori(0, count) as j:
                        copy_rows(m.ov, 0, j + 1)
                        expert(m.ov, j, 0, False)

                for tt in range(T):
                    dve.wait_ge([routing.gathered0, routing.gathered1][tt % 2], 64 * l + 32 * (tt // 2 + 1))
                    y = ygat[tt % 2]
                    link(dve.tensor_scalar(y[1], y[1], wts[:, 1, tt:tt + 1], None, ALU.mult))
                    link(dve.scalar_tensor_tensor(out=y[0], in0=y[0], scalar=wts[:, 0, tt:tt + 1], in1=y[1],
                                                  op0=ALU.mult, op1=ALU.add))
                    link(dve.scalar_tensor_tensor(out=h[:, tt, :], in0=h[:, tt, :], scalar=ALPHA if l < 2 else 1.0,
                                                  in1=y[0], op0=ALU.mult, op1=ALU.add))
                    dve.sem_inc(routing.summed, 1)

            mixture(0)
            layer_norm(par.ln1, tiles_written, turns["ffn0"].src0)
            link(dve.memset(uT[:, :, 0:PAD], 0.0))
            for i in range(2):
                link(dve.memset(win[i][:, :, 0:PAD], 0.0))
            for g in range(4):
                dve.wait_ge(po.u, 2 * g + 2)
                src = uT[:, 2 * g:2 * g + 2, :]
                width = 1
                for d in range(g + 1):
                    dst = win[d % 2]
                    link(dve.tensor_tensor(dst[:, :, PAD:], src[:, :, PAD:], src[:, :, PAD - width:PAD + S - width],
                                           ALU.add))
                    src, width = dst, 2 * width
                pg = pT[:, 2 * g:2 * g + 2, :]
                u_ = uT[:, 2 * g:2 * g + 2, PAD:]
                link(dve.scalar_tensor_tensor(out=pg, in0=src[:, :, PAD:], scalar=1.0 / width, in1=u_,
                                              op0=ALU.mult, op1=ALU.subtract))
                for k in range(2):
                    link(dve.tensor_tensor(pg[:, k, 0:PAD], src[:, k, PAD:2 * PAD],
                                           con[:, C_INV + PAD * g:C_INV + PAD * g + PAD], ALU.mult))
                    link(dve.tensor_tensor(pg[:, k, 0:PAD], pg[:, k, 0:PAD], u_[:, k, 0:PAD], ALU.subtract))
                dve.sem_inc(po.p, 1)
            residual(first["pout"], ALPHA)
            layer_norm(par.ln2, tiles_written, turns["mix1"].src0)
            mixture(1)
            layer_norm(par.ln3, ln3_done, 0)
            rms_norm(lnp[:, 0:D], par.rms0, hn, tiles_written, turns["rms0"].src0, 1e-6)
            def log1p(y, w, acc):
                link(dve.tensor_scalar(w, y, 2.0, None, ALU.add))
                link(dve.reciprocal(w, w))
                link(dve.tensor_tensor(y, y, w, ALU.mult))
                link(dve.tensor_tensor(w, y, y, ALU.mult))
                link(dve.tensor_scalar(acc, w, 1.0 / (2 * SERIES + 1), None, ALU.mult))
                for n in range(SERIES - 1, -1, -1):
                    link(dve.scalar_tensor_tensor(out=acc, in0=acc, scalar=1.0 / (2 * n + 1), in1=w if n else y,
                                                  op0=ALU.add, op1=ALU.mult))

            dve.wait_ge(par.conv, 128)
            lm, sy, sw, sacc, sp8 = convp[:, 28:32], spl[:, 0:4], spl[:, 4:8], spl[:, 8:12], spl[:, 12:16]
            link(dve.scalar_tensor_tensor(out=sy, in0=lm, scalar=-1.0, in1=lm, op0=ALU.mult, op1=ALU.min))
            dve.sem_inc(b2.sp_in, 1)
            dve.wait_ge(b2.sp_e, 1)
            log1p(sy, sw, sacc)
            link(dve.tensor_scalar(sp8, lm, -1.0, 0.0, ALU.mult, ALU.max))
            link(dve.scalar_tensor_tensor(out=sp8, in0=sacc, scalar=2.0, in1=sp8, op0=ALU.mult, op1=ALU.add))
            link(dve.tensor_scalar(sp8, sp8, 8.0, None, ALU.mult))
            for ch in range(4):
                dve.wait_ge(b2.copied, R_REC + ch + 1)
                link(dve.tensor_scalar(bx[:, ch, :], be[:, ch, :], taps[:, 3, ch:ch + 1], convp[:, 16 + ch:17 + ch],
                                       ALU.mult, ALU.add))
                for lag in range(1, 4):
                    ins = dve.scalar_tensor_tensor(out=bx[:, ch, lag:S], in0=be[:, ch, 0:S - lag],
                                                   scalar=taps[:, 3 - lag, ch:ch + 1], in1=bx[:, ch, lag:S],
                                                   op0=ALU.mult, op1=ALU.add)
                    if lag < 3:
                        link(ins)
                ins.then_inc(b2.conv, 1)
            dve.wait_ge(b2.copied, R_F + 1)
            dve.scalar_tensor_tensor(out=fb[1], in0=fb[0], scalar=-1.0, in1=fb[0], op0=ALU.mult, op1=ALU.min)\
                .then_inc(b2.f_in, 1)
            dve.wait_ge(b2.f_e, 1)
            log1p(fb[1], fb[2], fb[3])
            link(dve.tensor_scalar(fb[0], fb[0], 0.0, None, ALU.min))
            link(dve.scalar_tensor_tensor(out=fb[1], in0=fb[3], scalar=-2.0, in1=fb[0], op0=ALU.mult, op1=ALU.add))
            link(dve.memset(fb[2], 0.0))
            dve.tensor_tensor_scan(fb[0], fb[1], fb[2], 0.0, ALU.add, ALU.add).then_inc(b2.c, 1)
            for ch in range(4):
                dve.wait_ge(b2.copied, R_LRU + 2 * ch + 2)
                dve.tensor_scalar(br[:, ch, :], br[:, ch, :], sp8[:, ch:ch + 1], None, ALU.mult)\
                    .then_inc(b2.decay, 1)
                link(dve.tensor_tensor(bi[:, ch, :], bi[:, ch, :], bx[:, ch, :], ALU.mult))
            for ch in range(4):
                dve.wait_ge(b2.tau, ch + 1)
                link(dve.tensor_scalar(bx[:, ch, :], br[:, ch, :], 1.0, None, ALU.add))
                link(dve.reciprocal(bx[:, ch, :], bx[:, ch, :]))
                dve.scalar_tensor_tensor(out=br[:, ch, :], in0=br[:, ch, :], scalar=2.0, in1=bx[:, ch, :],
                                         op0=ALU.mult, op1=ALU.mult).then_inc(b2.m2, 1)
            for ch in range(4):
                dve.wait_ge(b2.mult, ch + 1)
                link(dve.tensor_tensor(bi[:, ch, :], bi[:, ch, :], br[:, ch, :], ALU.mult))
                link(dve.tensor_tensor_scan(bx[:, ch, :], be[:, ch, :], bi[:, ch, :], 0.0, ALU.mult, ALU.add))
            dve.wait_ge(units_used, first["v2"] + 2)
            for ch in range(4):
                dve.tensor_tensor(hT[:, 4 + ch, :], bx[:, ch, :], bg[:, ch, :], ALU.mult).then_inc(b2.lruT, 1)
            dve.wait_ge(b2.lruT, 4)
            dve.wait_ge(at.cq, 1)

            def logits2(g):
                hh, qb = g // 4, g % 4
                n, lg = P * (qb + 1), lg2[g % 2]
                dve.wait_ge(at.sc, 64 + g + 1)
                dve.wait_ge(at.ck, hh + 1)
                link(dve.scalar_tensor_tensor(out=lg[:, 0:n], in0=bank[g % 2][:, 0:n], scalar=cq[:, qb, hh:hh + 1],
                                              in1=nck[hh % 2][:, 0:n], op0=ALU.add, op1=ALU.add))
                link(dve.tensor_tensor(lg[:, P * qb:n], lg[:, P * qb:n], causal, ALU.add))
                link(dve.tensor_reduce(mx[:, g % 2:g % 2 + 1], lg[:, 0:n], AX, ALU.max))
                dve.tensor_scalar(negmax[:, g % 2:g % 2 + 1], mx[:, g % 2:g % 2 + 1], -1.0, None, ALU.mult)\
                    .then_inc(at.negmax, 1)

            def out2(g):
                hh, qb = g // 4, g % 4
                dve.wait_ge(at.av, 32 + g + 1)
                q = slice(g % 4, g % 4 + 1)
                link(dve.reciprocal(rr2[:, q], rs2[:, q]))
                dve.tensor_scalar(att2[:, qb, 64 * hh:64 * hh + 64], bank[4 + g % 2][:, 0:64], rr2[:, q], None,
                                  ALU.mult).then_inc(at.o, 1)

            logits2(0)
            for g in range(32):
                if g < 31:
                    logits2(g + 1)
                if g >= 1:
                    out2(g - 1)
            out2(31)
            dve.wait_ge(at.o, 64)
            dve.sem_inc(tiles_written, T)
            residual(first["out2"], 1.0)
            rms_norm(lnp[:, 0:D], par.rms1, hn, tiles_written, turns["rms1"].src0, 1e-6)
            mixture(2)
            rms_norm(lnp[:, D:2 * D], par.rms2, hn, out_ready, 0, 1e-6)

        @block.gpsimd
        def _(pool):
            def bcast(dst, src, s, n):
                pool.dma_start(dst, src.to_broadcast([P, n])).then_inc(s, 16)

            bcast(subg, t["attn_sub_g"], par.subg, 128)
            for i, n in enumerate(("attn_lq1", "attn_lk1", "attn_lq2", "attn_lk2")):
                bcast(lamv[:, i, :], t[n], par.lam, 64)

            def load_norm(s, layer, half, after, count):
                pool.wait_ge(after, count)
                bcast(lnp[:, 0:D], t["ln_g"][layer, half:half + 1, :], s, D)
                bcast(lnp[:, D:2 * D], t["ln_b"][layer, half:half + 1, :], s, D)

            load_norm(par.ln0, 0, 0, at.rope, 16)

            def mixture(l, src, before):
                m = moe[l]
                main = m.main()
                pool.wait_ge(tiles_written, turns[before].src_all)
                pool.dma_start(wr[:, :, 0:NG], router_g[l].rearrange("(k p) n -> p k n", p=P))\
                    .then_inc(routing.router_loaded, 16)
                if l < 2:
                    pool.dma_start(wr[:, :, NG:NG + E], t["moe_w_exp_router"][l].rearrange("(k p) n -> p k n", p=P))\
                        .then_inc(routing.router_loaded, 16)
                else:
                    for g in range(NG):
                        pool.dma_start(wr[:, :, NG + 8 * g:NG + 8 * g + 8],
                                       t["w_inner_2"][0, g].rearrange("(k p) n -> p k n", p=P))\
                            .then_inc(routing.router_loaded, 16)
                bcast(rbias[:, 0:NG], router_gb[l], routing.router_loaded, NG)
                bcast(rbias[:, NG:NG + E], router_eb[l], routing.router_loaded, E)
                if l == 0:
                    pool.wait_ge(rows_zeroed, 32)
                pool.wait_ge(routing.indices, m.l + 1)
                for k in range(2):
                    for tt in range(T):
                        pool.indirect_dma_start(
                            out=x_rows, out_offset=bass.IndirectOffsetOnAxis(ap=idx[:, T * k + tt:T * k + tt + 1], axis=0),
                            in_=src[:, tt, :], in_offset=None).then_inc(routing.scattered, 16)
                for s in range(2):
                    pool.wait_ge(main.y_stored[s], main.store0[s] + 32 * E // 2)
                count = pool.value_load(ovi[0:1, 16:17], min_val=0, max_val=OVF)
                with pool.If(count > 0):
                    pool.wait_ge(m.ov.y_stored[0], 32 * count)
                for tt in range(T):
                    if tt >= 2:
                        pool.wait_ge(routing.summed, T * l + tt - 1)
                    for k in range(2):
                        pool.indirect_dma_start(
                            out=ygat[tt % 2][k], out_offset=None, in_=y_rows,
                            in_offset=bass.IndirectOffsetOnAxis(ap=idx[:, T * k + tt:T * k + tt + 1], axis=0))\
                            .then_inc([routing.gathered0, routing.gathered1][tt % 2], 16)

            load_norm(par.ln1, 0, 1, tiles_written, turns["mix0"].src_all)
            mixture(0, h, "mix0")
            load_norm(par.ln2, 1, 0, tiles_written, turns["ffn0"].src_all)
            pool.dma_start(pscale, t["pool_scale"][0].rearrange("(k p) -> p k", p=P),
                           allow_slow_non_contiguous=True).then_inc(par.pscale, 16)
            load_norm(par.ln3, 1, 1, tiles_written, turns["mix1"].src_all)
            mixture(1, h, "mix1")
            pool.wait_ge(ln3_done, T)
            bcast(lnp[:, 0:D], t["mix_norm_2"], par.rms0, D)
            def vector(dst, src, s):
                pool.dma_start(dst, src.rearrange("a (c p) -> p (a c)", p=P), allow_slow_non_contiguous=True)\
                    .then_inc(s, 16)

            for i in range(4):
                vector(taps[:, i, :], t["conv_w_2"][0, i:i + 1, :], par.conv)
            vector(convp[:, 16:20], t["conv_b_2"], par.conv)
            vector(convp[:, 20:24], t["b_a_2"].rearrange("l n i -> l (n i)"), par.conv)
            vector(convp[:, 24:28], t["b_x_2"].rearrange("l n i -> l (n i)"), par.conv)
            vector(convp[:, 28:32], t["lru_lambda_2"], par.conv)
            pool.dma_start(wf, t["w_in_2"][0][:, 1536:1544].rearrange("(k p) n -> p k n", p=P))\
                .then_inc(par.wf, 16)
            pool.dma_start(bfg, t["b_forget_2"].rearrange("a n -> n a"), allow_slow_non_contiguous=True)\
                .then_inc(par.bf, 16)
            for a, n in enumerate(("w_a_2", "w_x_2")):
                for b in range(2):
                    pool.dma_start(wab[64 * b:64 * b + 64, a, :, :],
                                   t[n][0].rearrange("(c b) i j -> b i c j", b=2)[b]).then_inc(par.wab, 16)
            pool.wait_ge(at.ck, 8)
            bcast(lnp[:, 0:D], t["ffn_norm_2"], par.rms1, D)
            bcast(lnp[:, D:2 * D], t["final_norm_2"].unsqueeze(0), par.rms2, D)
            mixture(2, hn, "rms1")


_INS = ["x", "attn_w_qkv", "attn_w_o", "attn_lq1", "attn_lk1", "attn_lq2", "attn_lk2", "attn_sub_g", "pool_w_in",
        "pool_w_grp", "pool_scale", "pool_w_out", "ln_g", "ln_b", "moe_w_grp_router", "moe_b_grp_router",
        "moe_w_exp_router", "moe_b_exp_router", "moe_w_gate", "moe_w_up", "moe_w_down", "mix_norm_2", "w_in_2",
        "b_forget_2", "conv_w_2", "conv_b_2", "w_a_2", "b_a_2", "w_x_2", "b_x_2", "lru_lambda_2", "w_out_2",
        "ffn_norm_2", "w_group_2", "b_group_2", "w_inner_2", "b_inner_2", "w_gate_2", "w_up_2", "w_down_2",
        "final_norm_2"]


def constants():
    import numpy as np

    p = np.arange(P)
    con = np.zeros((P, C_W), np.float32)
    con[:, C_ID:C_ID + P] = np.eye(P)
    con[:, C_TRI:C_TRI + P] = p[:, None] < p[None, :]
    con[:, C_ONE:C_ONE + P] = 1
    con[:, C_CAUS:C_CAUS + P] = np.where(p[None, :] <= p[:, None], 0, -BIG)
    for q in range(P):
        if q % 64 < 16:
            con[q // 64 * 64 + (q % 64 + 8) % 16, C_ROPE + q] = 1
    con[:, C_IO:C_IO + E] = np.arange(E)
    con[:, C_GRP:C_GRP + E] = np.arange(E) // (E // NG)
    for g in range(4):
        con[:, C_INV + 16 * g:C_INV + 16 * g + 16] = np.float32(1) / np.minimum(np.arange(1, 17), 2 ** (g + 1))
    inv = np.float32(500000.0) ** (-np.arange(0, 16, 2, dtype=np.float32) / np.float32(16))
    ang = np.arange(S, dtype=np.float32)[:, None] * inv[None, :]
    cos, sin = np.cos(ang).T, np.sin(ang).T
    rope = np.zeros((P, 2, S), np.float32)
    rope[:, 0] = 1
    for m in range(2):
        b = 64 * m
        rope[b:b + 8, 0], rope[b + 8:b + 16, 0] = cos, cos
        rope[b:b + 8, 1], rope[b + 8:b + 16, 1] = -sin, sin
    return con, rope.reshape(P, 2 * S)


def kernel(**inputs):
    import numpy as _np
    import concourse.bacc as _bacc
    from concourse import mybir as _mybir
    from concourse.bass_utils import run_bass_kernel_spmd as _run

    nc = _bacc.Bacc("TRN2", target_bir_lowering=False, num_devices=1)
    arrays, aps = {}, {}
    con, rope = constants()
    for name, a in [(n, inputs[n]) for n in _INS] + [("con", con), ("rope", rope)]:
        a = _np.ascontiguousarray(a)
        arrays[f"in_{name}_dram"] = a
        aps[name] = nc.dram_tensor(f"in_{name}_dram", a.shape, _mybir.dt.from_np(a.dtype), kind="ExternalInput").ap()
    aps["out"] = nc.dram_tensor("out_0_dram", (1, S, D), _mybir.dt.float32, kind="ExternalOutput").ap()
    program(nc, aps)
    r = _run(nc, [arrays], core_ids=[0])
    return r.results[0]["out_0_dram"]
```

```python
import concourse.bass as bass
from concourse import mybir
from contextlib import ExitStack

D = 1024
S = 512
P = 128
T = S // P
K = D // P
E = 32
NG = 4
BLK = 64
MAIN = 64
OVF = 15
TURN = 4
UNITS = 12
UW = 2048
BIG = 1e30
ALPHA = 4.0 ** 0.25
LAMBDA_INIT = 0.8 - 0.6
FDIM = (512, 512, 256)

C_ID, C_TRI, C_ONE, C_CAUS, C_ROPE, C_IO, C_GRP, C_J, C_OB, C_INV, C_TH, C_SLOT, C_W = \
    0, 128, 256, 384, 512, 640, 672, 704, 720, 736, 800, 808, 872


def rank_thresholds():
    return [MAIN + BLK * k for k in range((S - MAIN + BLK - 1) // BLK)]


def weight_plan(w):
    units, first = [], {}

    def add(name, ap):
        first.setdefault(name, len(units))
        units.append(ap)

    def cols(name, ap, lo):
        add(name, ap[:, lo:lo + 256].rearrange("(k p) n -> p k n", p=P))

    def rows(name, ap, width):
        for n in range(width // 512):
            for kk in range(2):
                add(name, ap[512 * kk:512 * kk + 512, 512 * n:512 * n + 512].rearrange("(k p) n -> p k n", p=P))

    rows("v", w["qkv"][:, 2 * D:3 * D], D)
    for pair in range(4):
        cols("qk", w["qkv"], 256 * pair)
        cols("qk", w["qkv"], D + 256 * pair)
    rows("wo", w["wo"], D)
    first["moe0"] = len(units)
    units += [None] * (E * 6)
    for g in range(4):
        cols("pin", w["pin"], 256 * g)
    add("pgrp", w["pgrp"].rearrange("g (c p) n -> p (g c) n", p=P))
    rows("pout", w["pout"], D)
    first["moe1"] = len(units)
    units += [None] * (E * 6)
    for lo in (2056, 2312):
        cols("rec", w["in2"], lo)
    for lo in (1544, 1800):
        cols("gate", w["in2"], lo)
    for lo in (0, 256):
        cols("q2", w["in2"], lo)
    for lo in (512, 768):
        cols("k2", w["in2"], lo)
    rows("v2", w["in2"][:, 1024:1536], 512)
    rows("out2", w["out2"], D)
    first["moe2"] = len(units)
    return units, first


def program(nc, t):
    f32, u32 = mybir.dt.float32, mybir.dt.uint32
    ACT, ALU, AX = mybir.ActivationFunctionType, mybir.AluOpType, mybir.AxisListType.X
    w = {"qkv": t["attn_w_qkv"][0], "wo": t["attn_w_o"][0], "pin": t["pool_w_in"][0],
         "pgrp": t["pool_w_grp"][0], "pout": t["pool_w_out"][0], "in2": t["w_in_2"][0], "out2": t["w_out_2"][0]}
    units, first = weight_plan(w)
    experts = [[t[n][l] for n in ("moe_w_gate", "moe_w_up", "moe_w_down")] for l in range(2)]
    experts.append([t[n][0].rearrange("g e a b -> (g e) a b") for n in ("w_gate_2", "w_up_2", "w_down_2")])
    router_g = [t["moe_w_grp_router"][0], t["moe_w_grp_router"][1], t["w_group_2"][0]]
    router_gb = [t["moe_b_grp_router"][0:1], t["moe_b_grp_router"][1:2], t["b_group_2"][0:1]]
    router_eb = [t["moe_b_exp_router"][0:1], t["moe_b_exp_router"][1:2],
                 t["b_inner_2"].rearrange("l g e -> l (g e)")[0:1]]

    rows_ = (E + OVF + 2) * BLK
    rows_ += rows_ % P
    y_rows = nc.dram_tensor("y_rows", (rows_, D), f32, kind="Internal").ap()

    with ExitStack() as c:
        def sb(name, shape, dt=f32):
            return c.enter_context(nc.sbuf_tensor(name, shape, dt))

        def sem(name):
            return c.enter_context(nc.semaphore(name))

        con = sb("con", [P, C_W])
        ident, tri, ones = con[:, C_ID:C_ID + P], con[:, C_TRI:C_TRI + P], con[:, C_ONE:C_ONE + P]
        causal, rope_p = con[:, C_CAUS:C_CAUS + P], con[:, C_ROPE:C_ROPE + P]
        h = sb("h", [P, T, D])
        hT = sb("hT", [P, K, S])
        ring = [sb(f"ring{i}", [P, UW]) for i in range(UNITS)]
        work = sb("work", [P, 18432])
        small = sb("small", [P, 512])
        zeros = sb("zeros", [P, 256])
        idx = sb("idx", [P, 2 * T], u32)
        top8 = sb("top8", [P, 2 * T, 8], u32)
        ovi = sb("ovi", [P, 32], u32)
        bank = [c.enter_context(nc.psum_tensor(f"bank{i}", [P, 512], f32)) for i in range(8)]
        lnp = work[:, 16384:18432]

        def wk(lo, n, parts=(0, P)):
            return work[parts[0]:parts[1], lo:lo + n]

        def sm(lo, n, parts=(0, P)):
            return small[parts[0]:parts[1], lo:lo + n]

        unit_loaded = [sem(f"unit_loaded{i}") for i in range(UNITS)]
        units_used = sem("units_used")
        const_loaded, x_loaded = sem("const_loaded"), [sem(f"x_loaded{i}") for i in range(T)]
        half_unit = sem("half_unit")
        tile_done = sem("tile_done")
        out_ready, out_done = sem("out_ready"), sem("out_done")
        rows_zeroed, zero_ready = sem("rows_zeroed"), sem("zero_ready")
        dve_step = sem("dve_step")

        tiles_written, tiles_turned, tiles_copied = sem("tiles_written"), sem("tiles_turned"), sem("tiles_copied")

        class Turn:

            def __init__(self, src0, copied0, src_all, copied_all):
                self.src0, self.copied0, self.src_all, self.copied_all = src0, copied0, src_all, copied_all

        turns, written, copied = {}, 0, 0
        for name in ("x", "o1", "mix0", "ffn0", "mix1", "rms0", "att2", "rms1"):
            chunks = 4 if name == "att2" else K
            src0, copied0 = written, copied
            written += T if name != "x" else 0
            copied += T * chunks // 4
            turns[name] = Turn(src0, copied0, written, copied)

        class Parameters:

            def __init__(self):
                self.rope, self.subg, self.lam = sem("par_rope"), sem("par_subg"), sem("par_lam")
                self.ln0, self.ln1, self.ln2 = sem("par_ln0"), sem("par_ln1"), sem("par_ln2")
                self.ln3, self.pscale, self.rms0 = sem("par_ln3"), sem("par_pscale"), sem("par_rms0")
                self.conv, self.wab, self.wf = sem("par_conv"), sem("par_wab"), sem("par_wf")
                self.rms1, self.rms2, self.bf = sem("par_rms1"), sem("par_rms2"), sem("par_bf")

        class Steps:

            def __init__(self, name, buffers, used, base, first_row):
                self.slot, self.sel = sem(f"{name}_slot"), sem(f"{name}_sel")
                self.xt, self.xT, self.sg = sem(f"{name}_xt"), sem(f"{name}_xT"), sem(f"{name}_sg")
                self.hg, self.ht, self.hT = sem(f"{name}_hg"), sem(f"{name}_ht"), sem(f"{name}_hT")
                self.ysb = sem(f"{name}_ysb")
                self.y_stored = [sem(f"{name}_y_stored{i}") for i in range(buffers)]
                self.used, self.base, self.first_row = used, base, first_row
                self.at_mixture(0)

            def at_mixture(self, l):
                self.n0, self.x0, self.sel0 = E * l, (E + 2) * l, (E // 2 + 2) * l
                self.store0 = [32 * (E // 2) * l] * 2

        class Routing:

            def __init__(self):
                self.router_loaded, self.logits, self.exp_in = sem("moe_router_loaded"), sem("moe_logits"), sem("moe_exp_in")
                self.exp_out, self.onehots, self.ranks = sem("moe_exp_out"), sem("moe_onehots"), sem("moe_ranks")
                self.indices, self.gathered0 = sem("moe_indices"), sem("moe_gathered0")
                self.gathered1, self.summed = sem("moe_gathered1"), sem("moe_summed")

        class Mixture:
            def __init__(self, l):
                self.l, self.F, self.base = l, FDIM[l], first[f"moe{l}"]
                self.upb = 6 if self.F == 512 else 3
                self.ov_units = sem(f"ov{l}_units")
                self.ov = Steps(f"ov{l}", 1, sem(f"ov{l}_used"), 1, E)

            def main(self):
                steps.base = self.base
                steps.at_mixture(self.l)
                return steps

        routing = Routing()
        steps = Steps("main", 2, units_used, 0, 0)
        moe = [Mixture(l) for l in range(3)]

        class Attention:

            def __init__(self):
                self.v, self.raw, self.perm = sem("at_v"), sem("at_raw"), sem("at_perm")
                self.rope, self.sc, self.negmax = sem("at_rope"), sem("at_sc"), sem("at_negmax")
                self.exp, self.a, self.at = sem("at_exp"), sem("at_a"), sem("at_at")
                self.aT, self.av, self.o = sem("at_aT"), sem("at_av"), sem("at_o")
                self.lam_in, self.lam_ex, self.var = sem("at_lam_in"), sem("at_lam_ex"), sem("at_var")
                self.std, self.cqp, self.cq = sem("at_std"), sem("at_cqp"), sem("at_cq")
                self.ckp, self.ck = sem("at_ckp"), sem("at_ck")

        class Pooling:

            def __init__(self):
                self.u, self.p, self.g = sem("po_u"), sem("po_p"), sem("po_g")
                self.y = sem("po_y")

        class Second:

            def __init__(self):
                self.copied, self.conv, self.pairs = sem("b2_copied"), sem("b2_conv"), sem("b2_pairs")
                self.sp_in, self.sp_e, self.decay = sem("b2_sp_in"), sem("b2_sp_e"), sem("b2_decay")
                self.tau, self.m2, self.mult = sem("b2_tau"), sem("b2_m2"), sem("b2_mult")
                self.free, self.f, self.f_in = sem("b2_free"), sem("b2_f"), sem("b2_f_in")
                self.f_e, self.c, self.lruT = sem("b2_f_e"), sem("b2_c"), sem("b2_lruT")

        par, at, po, b2 = Parameters(), Attention(), Pooling(), Second()
        ln3_done = sem("ln3_done")
        norm_var, norm_std = sem("norm_var"), sem("norm_std")

        def waits(eng, step_sem):
            count = [0]

            def link(ins):
                count[0] += 1
                ins.then_inc(step_sem, 1)
                eng.wait_ge(step_sem, count[0])
            return link

        def wait_unit(eng, u):
            eng.wait_ge(unit_loaded[u % UNITS], 16 * (u // UNITS + 1))

        t_units = [u for n in ("qk", "pin", "rec", "gate", "q2", "k2")
                   for u in range(first[n], first[n] + {"qk": 8, "pin": 4}.get(n, 2))]
        b_halves = [first[n] + 2 * i for n, k in (("v", 2), ("wo", 2), ("pout", 2), ("v2", 1), ("out2", 2))
                    for i in range(k)]

        def wait_half(eng, u, half):
            if half:
                eng.wait_ge(units_used, u + 1)
            else:
                eng.wait_ge(half_unit, t_units.index(u) + 1)

        def wait_tile(eng, u, tt):
            if tt == T - 1:
                eng.wait_ge(units_used, u + 2)
            else:
                eng.wait_ge(tile_done, 3 * b_halves.index(u) + tt + 1)

        def over_blocks(eng, body):
            for s in range(TURN):
                body(0, s)
            with eng.Fori(1, E // TURN) as i:
                for s in range(TURN):
                    body(i, s)

        sel = [wk(512 * i, 512).rearrange("p (t n) -> p t n", t=T) for i in range(2)]
        xgT = [wk(1024 + 1024 * i, 1024).rearrange("p (k n) -> p k n", k=K) for i in range(2)]
        pos = wk(7572, T * (E + 4)).rearrange("p (t n) -> p t n", t=T)
        rowA = wk(7716, T * E).rearrange("p (t n) -> p t n", t=T)
        oslot = wk(7844, T)
        sg, hg = wk(3072, 512, (BLK, P)), wk(3584, 512, (BLK, P))
        hgT = wk(4096, 256)
        ysb = [wk(4352 + 512 * i, 512) for i in range(2)]
        wr = wk(5376, 288).rearrange("p (k n) -> p k n", k=K)
        rbias = wk(5664, 36)
        logit = wk(5700, 144).rearrange("p (t n) -> p t n", t=T)
        gpad = wk(5844, 32).rearrange("p (t n) -> p t n", t=T)
        g8 = wk(5876, 32).rearrange("p (t n) -> p t n", t=T)
        e8 = wk(5908, 32).rearrange("p (t n) -> p t n", t=T)
        emask = wk(5940, 128).rearrange("p (t n) -> p t n", t=T)
        em = wk(6068, 128).rearrange("p (t n) -> p t n", t=T)
        hot1 = wk(6196, 128).rearrange("p (t n) -> p t n", t=T)
        hot2 = wk(6324, 128).rearrange("p (t n) -> p t n", t=T)
        hots = wk(6452, 128).rearrange("p (t n) -> p t n", t=T)
        rank = wk(6580, 128).rearrange("p (t n) -> p t n", t=T)
        rowE = wk(6708, 128).rearrange("p (t n) -> p t n", t=T)
        nblk, ovend, ovdiff, zero32 = (wk(6836 + 32 * i, 32) for i in range(4))
        ovcmp = wk(6964, 512).rearrange("p (j n) -> p j n", j=16)

        def over_tiles(v, n):
            return v.unsqueeze(1).to_broadcast([P, T, n])

        def over_last(v, n):
            return v.unsqueeze(2).to_broadcast([P, v.shape[1], n])

        ovf = wk(7476, 17)
        tokf = wk(7500, 64)
        wts = wk(7564, 8).rearrange("p (k t) -> p k t", k=2)
        ygat = [[wk(8192 + 2048 * i + 1024 * k, 1024) for k in range(2)] for i in range(2)]
        hn = wk(12288, 4096).rearrange("p (t d) -> p t d", t=T)
        GU, DN, XT, HT, RT, CT = bank[0], bank[1], [bank[2], bank[6]], bank[3], bank[4], bank[5]

        v1 = wk(0, 4096).rearrange("p (t d) -> p t d", t=T)
        o1 = wk(4096, 4096).rearrange("p (t d) -> p t d", t=T)
        qT = [wk(8192 + 512 * i, 512) for i in range(4)]
        kT = [wk(10240 + 512 * i, 512) for i in range(4)]
        prob = [wk(12288 + 512 * i, 512) for i in range(2)]
        abuf = [wk(13312 + 512 * i, 512) for i in range(2)]
        aT = wk(14336, 512)
        raw = [wk(14848 + 512 * i, 512) for i in range(2)]
        rtmp = wk(15872, 512)
        ropec, ropes = wk(16384, 512), wk(16896, 512)
        subg = sm(0, 128)
        lamv = sm(128, 256).rearrange("p (a n) -> p a n", a=4)
        stats = sm(384, 12).rearrange("p (a n) -> p a n", a=2)
        mv = sm(396, 8).rearrange("p (t n) -> p t n", t=T)
        rstd = sm(404, 4)
        mx, negmax = sm(408, 2), sm(410, 2)
        rs, rr = sm(412, 2), sm(414, 2)
        lam = sm(416, 4)
        sumsq = sm(420, 32).rearrange("p (t n) -> p t n", t=T)
        orstd = sm(452, 32).rearrange("p (t n) -> p t n", t=T)
        ojunk = sb("ojunk", [P, P])[:, :]

        PAD = 16
        uT = wk(0, K * (S + PAD)).rearrange("p (k n) -> p k n", k=K)
        win = [wk(4224 + 1056 * i, 1056).rearrange("p (k n) -> p k n", k=2) for i in range(2)]
        pT = wk(6336, 4096).rearrange("p (k n) -> p k n", k=K)
        yT = wk(10432, 4096).rearrange("p (k n) -> p k n", k=K)
        pscale = sm(0, 8)

        def quad(lo):
            return wk(lo, 2048).rearrange("p (k n) -> p k n", k=4)

        bx, br, bi, bg, be = (quad(2048 * i) for i in range(5))
        q2T, k2T, v2 = quad(10240), quad(12288), quad(14336)
        fb = [wk(lo, 512, (0, 8)) for lo in (16384, 16896, 17920, 14336)]
        lg2, p2T, nck = [wk(0 + 512 * i, 512) for i in range(2)], wk(1024, 512), [wk(1536 + 512 * i, 512) for i in range(2)]
        att2 = wk(4096, 2048).rearrange("p (t d) -> p t d", t=T)
        p2 = [wk(2560 + 512 * i, 512) for i in range(2)]
        wab = wk(17408, 512).rearrange("p (a c n) -> p a c n", a=2, c=4)
        convp = sm(0, 32)
        wf = sm(32, 64).rearrange("p (k n) -> p k n", k=K)
        bfg = sm(96, 1, (0, 8))
        spl = sm(100, 20)
        cq = sm(128, 32).rearrange("p (t n) -> p t n", t=T)
        rs2, rr2 = sm(160, 4), sm(164, 4)
        taps = convp[:, 0:16].rearrange("p (w c) -> p w c", w=4)
        SERIES = 8
        R_REC, R_GATE, R_F, R_Q, R_LRU, R_K, R_V, R_END = 0, 4, 8, 9, 13, 21, 25, 29

        block = c.enter_context(nc.Block())

        @block.sync
        def _(sp):
            def load(u):
                if u >= UNITS:
                    sp.wait_ge(units_used, u - UNITS + 1)
                sp.dma_start(ring[u % UNITS][:, :], units[u]).then_inc(unit_loaded[u % UNITS], 16)

            def expert_units(m, l, e):
                gate, up, down = experts[l]
                if m.F == 512:
                    for kk in range(2):
                        for a in (gate, up):
                            yield a[e, 512 * kk:512 * kk + 512, :].rearrange("(k p) n -> p k n", p=P)
                    for kk in range(2):
                        yield down[e, 256 * kk:256 * kk + 256, :].rearrange("(k p) n -> p k n", p=P)
                else:
                    for a in (gate, up):
                        yield a[e].rearrange("(k p) n -> p k n", p=P)
                    yield down[e].rearrange("(k p) n -> p k n", p=P)

            def mixture(l):
                m = moe[l]

                def body(i, s):
                    for q, src in enumerate(expert_units(m, l, TURN * i + s)):
                        u = m.base + m.upb * s + q
                        sp.wait_ge(units_used, u - UNITS + 1 + TURN * m.upb * i)
                        sp.dma_start(ring[u % UNITS][:, :], src).then_inc(unit_loaded[u % UNITS], 16)

                over_blocks(sp, body)
                sp.wait_ge(routing.indices, l + 1)
                count = sp.value_load(ovi[0:1, 16:17], min_val=0, max_val=OVF)
                with sp.If(count > 0):
                    sp.wait_ge(units_used, m.base + E * m.upb)
                    sp.sem_inc(m.ov.used, 1)
                    with sp.Fori(0, count) as j:
                        e = sp.value_load(ovi[0:1, bass.ds(j, 1)], min_val=0, max_val=E - 1)
                        sp.wait_ge(m.ov.used, m.upb * j + 1)
                        for q, src in enumerate(expert_units(m, l, e)):
                            u = m.base + q
                            sp.dma_start(ring[u % UNITS][:, :], src).then_inc(m.ov_units, 16)

            sp.dma_start(con[:, :], t["con"]).then_inc(const_loaded, 16)
            for i in range(T):
                sp.dma_start(h[:, i, :], t["x"][0, P * i:P * i + P, :]).then_inc(x_loaded[i], 16)
            sp.dma_start(work[:, 16384:17408], t["rope"]).then_inc(par.rope, 16)
            for u in range(first["wo"]):
                load(u)
            sp.wait_ge(zero_ready, 1)
            sp.dma_start(y_rows[E * BLK:rows_].rearrange("(p n) (q c) -> p (n q) c", p=P, c=256),
                         zeros[:, :].unsqueeze(1).to_broadcast([P, (rows_ - E * BLK) // P * 4, 256]))\
                .then_inc(rows_zeroed, 16)
            for u in range(first["wo"], first["moe0"]):
                load(u)
            mixture(0)
            for u in range(first["pin"], first["moe1"]):
                load(u)
            mixture(1)
            for u in range(first["rec"], first["moe2"]):
                load(u)
            mixture(2)

            for tt in range(T):
                sp.wait_ge(out_ready, tt + 1)
                sp.dma_start(t["out"][0, P * tt:P * tt + P, :], hn[:, tt, :]).then_inc(out_done, 16)
            sp.wait_ge(out_done, 16 * T)

        @block.tensor
        def _(pe):
            def project_t(u, banks, half, ks=range(K)):
                v = ring[u % UNITS][:, :].rearrange("p (k n) -> p k n", k=K)
                for k in ks:
                    mm = pe.matmul(banks[:, :], v[:, k, 128 * half:128 * half + 128], hT[:, k, :],
                                   start=(k == 0), stop=(k == K - 1))
                    if k == K - 1:
                        mm.then_inc(units_used if half else half_unit, 1)

            def project_b(u, operand, banks):
                for kk in range(2):
                    wait_unit(pe, u + kk)
                    v = ring[(u + kk) % UNITS][:, :].rearrange("p (k n) -> p k n", k=4)
                    for tt in range(T):
                        for k in range(4):
                            mm = pe.matmul(banks[tt][:, :], operand[:, 4 * kk + k, P * tt:P * tt + P], v[:, k, :],
                                           start=(kk + k == 0), stop=(kk + k == 4))
                        if tt == T - 1:
                            mm.then_inc(units_used, 1)
                        elif kk == 1:
                            mm.then_inc(tile_done, 1)

            def turn(name, src, chunks=K):
                s = turns[name]
                for tt in range(T):
                    if name == "x":
                        pe.wait_ge(x_loaded[tt], 16)
                    else:
                        pe.wait_ge(tiles_written, s.src0 + tt + 1)
                    for kk in range(chunks // 4):
                        for k in range(4):
                            mm = pe.transpose(bank[(2 * tt + kk) % 8][:, P * k:P * k + P],
                                              src[:, tt, P * (4 * kk + k):P * (4 * kk + k) + P], ident)
                        mm.then_inc(tiles_turned, 1)

            pe.wait_ge(const_loaded, 16)
            turn("x", h)
            pe.wait_ge(tiles_copied, turns["x"].copied_all)
            for n in range(2):
                project_b(first["v"] + 2 * n, hT, bank[4 * n:4 * n + 4])

            def chunk_unit(cc):
                pair, n = cc // 4, cc % 4
                return first["qk"] + 2 * pair + n // 2, n % 2

            def head_place(hh):
                return qT[hh % 4], kT[hh % 4]

            def scores(g):
                hh, qb = g // 4, g % 4
                if qb == 0:
                    pe.wait_ge(at.rope, 4 * (hh // 2) + 3 + hh % 2)
                q_, k_ = head_place(hh)
                for m in range(2):
                    rows = slice(64 * m, 64 * m + 64)
                    pe.matmul(bank[2 + 2 * (g % 2) + m][:, 0:P * (qb + 1)], q_[rows, P * qb:P * qb + P],
                              k_[rows, 0:P * (qb + 1)], start=True, stop=True).then_inc(at.sc, 1)

            def values(g):
                hh, qb = g // 4, g % 4
                pe.wait_ge(at.a, g + 1)
                for b in range(qb + 1):
                    mm = pe.transpose(bank[6][:, P * b:P * b + P], abuf[g % 2][:, P * b:P * b + P], ident)
                mm.then_inc(at.at, 1)
                pe.wait_ge(at.aT, g + 1)
                for b in range(qb + 1):
                    mm = pe.matmul(bank[7][:, 0:P], aT[:, P * b:P * b + P], v1[:, b, P * hh:P * hh + P],
                                   start=(b == 0), stop=(b == qb))
                mm.then_inc(at.av, 1)

            def permute(cc):
                pe.wait_ge(at.raw, cc + 1)
                pe.matmul(bank[cc % 2][:, :], rope_p, raw[cc % 2], start=True, stop=True).then_inc(at.perm, 1)

            pe.wait_ge(at.v, 2 * T)
            for step in range(5 * 8):
                pair, st = step // 8, step % 8
                if pair < 4:
                    cc = 4 * pair + st // 2
                    u, half = chunk_unit(cc)
                    if st % 2 == 0:
                        if cc >= 2:
                            pe.wait_ge(at.rope, cc - 1)
                        wait_unit(pe, u)
                    project_t(u, bank[cc % 2], half, range(4 * (st % 2), 4 * (st % 2) + 4))
                if pair >= 1:
                    scores(step - 8)
                if st % 2 == 0 and 1 <= 4 * pair + st // 2 <= 16:
                    permute(4 * pair + st // 2 - 1)
                if step > 8:
                    values(step - 9)
            values(31)
            turn("o1", o1)
            pe.wait_ge(tiles_copied, turns["o1"].copied_all)
            for n in range(2):
                project_b(first["wo"] + 2 * n, hT, bank[4 * n:4 * n + 4])
            turn("mix0", h)

            def mixture(l, before, src):
                m = moe[l]
                main = m.main()
                F, half_f = m.F, m.F // 128
                pe.wait_ge(tiles_copied, turns[before].copied_all)
                pe.wait_ge(routing.router_loaded, 64 * l + (64 if l < 2 else 112))
                for tt in range(T):
                    for k in range(K):
                        mm = pe.matmul(RT[:, 36 * tt:36 * tt + 36], hT[:, k, P * tt:P * tt + P], wr[:, k, :],
                                       start=(k == 0), stop=(k == K - 1))
                mm.then_inc(routing.logits, 1)
                pe.wait_ge(routing.onehots, l + 1)
                for tt in range(T):
                    for t0 in range(tt + 1):
                        mm = pe.matmul(CT[:, 32 * tt:32 * tt + 32], tri if t0 == tt else ones, hots[:, t0, :],
                                       start=(t0 == 0), stop=(t0 == tt))
                for t0 in range(T):
                    mm = pe.matmul(CT[:, 128:160], ones, hots[:, t0, :], start=(t0 == 0), stop=(t0 == T - 1))
                mm.then_inc(routing.ranks, 1)

                def turn_block(k, out, rows, eye):
                    if k == 0:
                        return pe.matmul(out, rows, eye, start=True, stop=True)
                    return pe.transpose(out, rows, eye)

                def turn_rows(b, buf, half, width):
                    for k in range(4):
                        for tt in range(T):
                            c0 = P * (4 * half + k)
                            mm = pe.matmul(XT[half][:, P * k:P * k + width], src[:, tt, c0:c0 + P],
                                           sel[buf][:, tt, 0:width], start=(tt == 0), stop=(tt == T - 1))
                    mm.then_inc(b.xt, 1)

                def expert(b, j, xT_, turned_, unit, need, ahead):
                    pe.wait_ge(b.xT, b.x0 + turned_)
                    if F == 512:
                        for kk in range(2):
                            need(2 * kk)
                            need(2 * kk + 1)
                            for k in range(4):
                                for a in range(2):
                                    v = unit(2 * kk + a).rearrange("p (k n) -> p k n", k=4)
                                    mm = pe.matmul(GU[BLK * a:BLK * a + BLK, :], xT_[:, 4 * kk + k, :], v[:, k, :],
                                                   start=(kk + k == 0), stop=(kk + k == 4))
                            mm.then_inc(b.used, 2)
                    else:
                        need(0)
                        need(1)
                        for k in range(K):
                            for a in range(2):
                                v = unit(a).rearrange("p (k n) -> p k n", k=K)
                                mm = pe.matmul(GU[BLK * a:BLK * a + BLK, 0:F], xT_[:, k, :], v[:, k, :],
                                               start=(k == 0), stop=(k == K - 1))
                        mm.then_inc(b.used, 2)
                    if ahead is not None:
                        ahead()
                    pe.wait_ge(b.hg, b.n0 + j + 1)
                    for k in range(half_f):
                        mm = turn_block(k, HT[:, BLK * k:BLK * k + BLK], hg[:, P * k:P * k + P], ident[BLK:P, BLK:P])
                    mm.then_inc(b.ht, 1)
                    pe.wait_ge(b.hT, b.n0 + j + 1)
                    hT_ = hgT.rearrange("p (k n) -> p k n", k=4)
                    for kk in range(F // 256):
                        need(m.upb - F // 256 + kk)
                        v = unit(m.upb - F // 256 + kk).rearrange("p (k n) -> p k n", k=2)
                        for k in range(2):
                            for n in range(2):
                                mm = pe.matmul(DN[BLK * n:BLK * n + BLK, :], hT_[:, 2 * kk + k, :],
                                               v[:, k, 512 * n:512 * n + 512],
                                               start=(kk + k == 0), stop=(2 * kk + k == half_f - 1))
                        mm.then_inc(b.used, 1)

                pe.wait_ge(main.sel, main.sel0 + 1)
                turn_rows(main, 0, 0, P)
                turn_rows(main, 0, 1, P)

                def body(i, s):
                    pair, of_pair = s // 2, s % 2

                    def unit(q):
                        return ring[(m.base + m.upb * s + q) % UNITS][:, :]

                    def need(q):
                        u = m.base + m.upb * s + q
                        pe.wait_ge(unit_loaded[u % UNITS], 16 * (u // UNITS + 1) + 16 * (TURN * m.upb // UNITS) * i)

                    def ahead():
                        if of_pair == 0:
                            pe.wait_ge(main.sel, main.sel0 + TURN // 2 * i + pair + 2)
                        turn_rows(main, (pair + 1) % 2, of_pair, P)

                    expert(main, TURN * i + s, xgT[pair % 2][:, :, BLK * of_pair:BLK * of_pair + BLK],
                           TURN * i + 2 * pair + 2, unit, need, ahead)
                over_blocks(pe, body)

                pe.wait_ge(routing.indices, m.l + 1)
                count = pe.value_load(ovi[0:1, 16:17], min_val=0, max_val=OVF)
                with pe.If(count > 0):
                    with pe.Fori(0, count) as j:
                        pe.wait_ge(m.ov.sel, j + 1)
                        turn_rows(m.ov, 0, 0, BLK)
                        turn_rows(m.ov, 0, 1, BLK)
                        expert(m.ov, j, xgT[0][:, :, 0:BLK], 2 * j + 2, lambda q: ring[(m.base + q) % UNITS][:, :],
                               lambda q: pe.wait_ge(m.ov_units, 16 * m.upb * j + 16 * m.upb), None)

            mixture(0, "mix0", h)
            turn("ffn0", h)
            pe.wait_ge(tiles_copied, turns["ffn0"].copied_all)
            for u in range(4):
                wait_unit(pe, first["pin"] + u)
                for half in range(2):
                    project_t(first["pin"] + u, bank[2 * u + half], half)
            u = first["pgrp"]
            wait_unit(pe, u)
            v = ring[u % UNITS][:, :].rearrange("p (k n) -> p k n", k=K)
            for g in range(4):
                pe.wait_ge(po.p, g + 1)
                for half in range(2):
                    for k in range(2):
                        mm = pe.matmul(bank[2 * g + half][:, :], v[:, 2 * g + k, P * half:P * half + P],
                                       pT[:, 2 * g + k, :], start=(k == 0), stop=(k == 1))
                    if g < 3 or half == 0:
                        mm.then_inc(po.g, 1)
            mm.then_inc(units_used, 1)
            pe.wait_ge(po.y, K)
            for n in range(2):
                project_b(first["pout"] + 2 * n, yT, bank[4 * n:4 * n + 4])
            turn("mix1", h)
            mixture(1, "mix1", h)
            turn("rms0", hn)
            def bank_of(r):
                if r >= 8:
                    pe.wait_ge(b2.copied, r - 7)
                return bank[r % 8]

            def results(name, r):
                for u in range(first[name], first[name] + 2):
                    wait_unit(pe, u)
                    for half in range(2):
                        project_t(u, bank_of(r), half)
                        r += 1

            pe.wait_ge(tiles_copied, turns["rms0"].copied_all)
            results("rec", R_REC)
            results("gate", R_GATE)
            pe.wait_ge(par.wf, 16)
            bk = bank_of(R_F)
            for k in range(K):
                mm = pe.matmul(bk[0:8, :], wf[:, k, :], hT[:, k, :], start=(k == 0), stop=(k == K - 1))
            mm.then_inc(b2.f, 1)
            results("q2", R_Q)
            pe.wait_ge(par.wab, 64)
            for ch in range(4):
                pe.wait_ge(b2.conv, ch + 1)
                for a in range(2):
                    bk = bank_of(R_LRU + 2 * ch + a)
                    for b in range(2):
                        half = slice(64 * b, 64 * b + 64)
                        mm = pe.matmul(bk[half, :], wab[half, a, ch, :], bx[half, ch, :], start=True, stop=True)
                    mm.then_inc(b2.pairs, 1)
            results("k2", R_K)
            pe.wait_ge(b2.copied, R_V - 8 + 4)
            project_b(first["v2"], hT, [bank[(R_V + tt) % 8] for tt in range(T)])
            pe.wait_ge(b2.copied, R_END)
            pe.wait_ge(b2.c, 1)
            for tt in range(T):
                mm = pe.transpose(bank[7][:, 8 * tt:8 * tt + 8], fb[0][:, P * tt:P * tt + P], ident[0:8, 0:8])
            mm.then_inc(at.cqp, 1)
            pe.wait_ge(at.cq, 1)

            def spread_c(hh):
                if hh >= 2:
                    pe.wait_ge(at.ck, hh - 1)
                pe.matmul(bank[6 + hh % 2][:, :], ident[0:8, hh:hh + 1].to_broadcast([8, P]), fb[0],
                          start=True, stop=True).then_inc(at.ckp, 1)

            def scores2(g):
                hh, qb = g // 4, g % 4
                half = slice(64 * (hh % 2), 64 * (hh % 2) + 64)
                pe.matmul(bank[g % 2][:, 0:P * (qb + 1)], q2T[half, hh // 2, P * qb:P * qb + P],
                          k2T[half, hh // 2, 0:P * (qb + 1)], start=True, stop=True).then_inc(at.sc, 1)

            def values2(g):
                hh, qb = g // 4, g % 4
                pe.wait_ge(at.exp, 64 + g + 1)
                for b in range(qb + 1):
                    mm = pe.transpose(bank[2 + g % 2][:, P * b:P * b + P], p2[g % 2][:, P * b:P * b + P], ident)
                mm.then_inc(at.at, 1)
                if g >= 2:
                    pe.wait_ge(at.o, 32 + g - 1)
                pe.wait_ge(at.aT, 32 + g + 1)
                for b in range(qb + 1):
                    mm = pe.matmul(bank[4 + g % 2][:, 0:64], p2T[:, P * b:P * b + P], v2[:, b, 64 * hh:64 * hh + 64],
                                   start=(b == 0), stop=(b == qb))
                mm.then_inc(at.av, 1)

            spread_c(0)
            scores2(0)
            for g in range(32):
                if g < 31:
                    scores2(g + 1)
                if g % 4 == 1 and g < 28:
                    spread_c(g // 4 + 1)
                values2(g)
            turn("att2", att2, 4)
            pe.wait_ge(tiles_copied, turns["att2"].copied_all)
            pe.wait_ge(b2.lruT, 4)
            for n in range(2):
                project_b(first["out2"] + 2 * n, hT, bank[4 * n:4 * n + 4])
            turn("rms1", hn)
            mixture(2, "rms1", hn)

        @block.scalar
        def _(act):
            def turned(name, chunks=K):
                s = turns[name]
                for tt in range(T):
                    for kk in range(chunks // 4):
                        n = chunks // 4 * tt + kk + 1
                        act.wait_ge(tiles_turned, s.copied0 + n)
                        act.activation(hT[:, 4 * kk:4 * kk + 4, P * tt:P * tt + P],
                                       bank[(2 * tt + kk) % 8][:, :].rearrange("p (k n) -> p k n", k=4),
                                       ACT.Copy).then_inc(tiles_copied, 1)

            norms = [0]

            def norm_root():
                norms[0] += 1
                act.wait_ge(norm_var, norms[0])
                act.activation(rstd, rstd, ACT.Sqrt).then_inc(norm_std, 1)

            turned("x")
            for n in range(2):
                for tt in range(T):
                    wait_tile(act, first["v"] + 2 * n, tt)
                    act.activation(v1[:, tt, 512 * n:512 * n + 512], bank[4 * n + tt][:, :], ACT.Copy)\
                       .then_inc(at.v, 1)

            act.wait_ge(at.lam_in, 1)
            act.activation(lam[:, 0:2], lam[:, 0:2], ACT.Exp).then_inc(at.lam_ex, 1)

            def copy_turned(g):
                act.wait_ge(at.at, g + 1)
                act.activation(aT[:, 0:P * (g % 4 + 1)], bank[6][:, 0:P * (g % 4 + 1)], ACT.Copy).then_inc(at.aT, 1)

            def copy_out(g):
                hh, qb = g // 4, g % 4
                act.wait_ge(at.av, g + 1)
                act.activation(o1[:, qb, P * hh:P * hh + P], bank[7][:, 0:P], ACT.Copy)
                act.activation(ojunk, bank[7][:, 0:P], ACT.Square, accum_out=sumsq[:, qb, hh:hh + 1])\
                   .then_inc(at.o, 1)

            for step in range(5 * 8 + 1):
                if step > 8:
                    copy_turned(step - 9)
                if 8 <= step < 40:
                    g = step - 8
                    for m in range(2):
                        act.wait_ge(at.negmax, 2 * g + m + 1)
                        n = P * (g % 4 + 1)
                        act.activation(prob[m][:, 0:n], bank[2 + 2 * (g % 2) + m][:, 0:n], ACT.Exp,
                                       bias=negmax[:, m:m + 1], scale=0.125, accum_out=rs[:, m:m + 1])\
                           .then_inc(at.exp, 1)
                if step > 8:
                    copy_out(step - 9)
                if step < 32 and step % 2:
                    cc = step // 2
                    pair, n = cc // 4, cc % 4
                    wait_half(act, first["qk"] + 2 * pair + n // 2, n % 2)
                    act.activation(raw[cc % 2], bank[cc % 2][:, :], ACT.Copy).then_inc(at.raw, 1)
            act.wait_ge(at.var, 1)
            act.activation(orstd, orstd, ACT.Sqrt).then_inc(at.std, 1)
            turned("o1")
            norm_root()
            turned("mix0")

            def mixture(l):
                m = moe[l]
                main = m.main()
                F = m.F
                act.wait_ge(routing.exp_in, l + 1)
                act.activation(tokf[:, 20:40], tokf[:, 0:20], ACT.Exp).then_inc(routing.exp_out, 1)

                def expert(b, j, s, reuse):
                    act.wait_ge(b.used, b.base + m.upb * j + m.upb - F // 256)
                    act.activation(sg[:, 0:F], GU[0:BLK, 0:F], ACT.Silu).then_inc(b.sg, 1)
                    act.wait_ge(b.used, b.base + m.upb * j + m.upb)
                    if reuse is not None:
                        act.wait_ge(b.y_stored[s], b.store0[s] + reuse)
                    act.activation(ysb[s], DN[:, :], ACT.Copy).then_inc(b.ysb, 1)
                    act.wait_ge(b.ysb, b.n0 + j + 1)
                    block_row = j + b.first_row
                    for n in range(2):
                        act.dma_start(y_rows[bass.ts(block_row, BLK), 512 * n:512 * n + 512],
                                      ysb[s][BLK * n:BLK * n + BLK, :]).then_inc(b.y_stored[s], 16)

                def body(i, s):
                    first_turn = type(i) is int
                    reuse = None if first_turn and s < 2 and l == 0 else 32 * (s // 2) + 16 * TURN * i
                    expert(main, TURN * i + s, s % 2, reuse)
                over_blocks(act, body)
                act.wait_ge(routing.indices, m.l + 1)
                count = act.value_load(ovi[0:1, 16:17], min_val=0, max_val=OVF)
                with act.If(count > 0):
                    for s in range(2):
                        act.wait_ge(main.y_stored[s], main.store0[s] + 32 * E // 2)
                    with act.Fori(0, count) as j:
                        expert(m.ov, j, 0, None)
                        act.wait_ge(m.ov.y_stored[0], 32 * j + 32)

            mixture(0)
            norm_root()
            turned("ffn0")
            for r in range(K):
                wait_half(act, first["pin"] + r // 2, r % 2)
                act.activation(uT[:, r, PAD:PAD + S], bank[r][:, :], ACT.Copy).then_inc(po.u, 1)
            act.wait_ge(par.pscale, 16)
            for r in range(K):
                if r < K - 1:
                    act.wait_ge(po.g, r + 1)
                else:
                    act.wait_ge(units_used, first["pgrp"] + 1)
                act.activation(yT[:, r, :], bank[r][:, :], ACT.Copy, scale=pscale[:, r:r + 1]).then_inc(po.y, 1)
            norm_root()
            turned("mix1")
            mixture(1)
            norm_root()
            norm_root()
            turned("rms0")
            def copy_result(dst, r, func=ACT.Copy, rows=P, **kw):
                act.activation(dst, bank[r % 8][0:rows, :], func, **kw).then_inc(b2.copied, 1)

            act.wait_ge(b2.sp_in, 1)
            act.activation(spl[:, 0:4], spl[:, 0:4], ACT.Exp).then_inc(b2.sp_e, 1)
            for r in range(4):
                wait_half(act, first["rec"] + r // 2, r % 2)
                copy_result(be[:, r, :], R_REC + r)
            for r in range(4):
                wait_half(act, first["gate"] + r // 2, r % 2)
                copy_result(bg[:, r, :], R_GATE + r, ACT.Gelu_apprx_tanh)
            act.wait_ge(b2.f, 1)
            act.wait_ge(par.bf, 16)
            copy_result(fb[0], R_F, ACT.Identity, 8, bias=bfg)
            for r in range(4):
                wait_half(act, first["q2"] + r // 2, r % 2)
                copy_result(q2T[:, r, :], R_Q + r, scale=0.125)
            act.wait_ge(b2.f_in, 1)
            act.activation(fb[1], fb[1], ACT.Exp).then_inc(b2.f_e, 1)
            for ch in range(4):
                for a in range(2):
                    act.wait_ge(b2.pairs, 2 * ch + a + 1)
                    copy_result((br, bi)[a][:, ch, :], R_LRU + 2 * ch + a, ACT.Sigmoid,
                                bias=convp[:, 20 + 4 * a + ch:21 + 4 * a + ch])
            for ch in range(4):
                act.wait_ge(b2.decay, ch + 1)
                act.activation(be[:, ch, :], br[:, ch, :], ACT.Exp, scale=-1.0).then_inc(b2.free, 1)
            act.wait_ge(b2.free, 4)
            for ch in range(4):
                act.activation(br[:, ch, :], br[:, ch, :], ACT.Tanh).then_inc(b2.tau, 1)
            for r in range(4):
                wait_half(act, first["k2"] + r // 2, r % 2)
                copy_result(k2T[:, r, :], R_K + r)
            for ch in range(4):
                act.wait_ge(b2.m2, ch + 1)
                act.activation(br[:, ch, :], br[:, ch, :], ACT.Sqrt).then_inc(b2.mult, 1)
            act.wait_ge(b2.c, 1)
            for tt in range(T):
                wait_tile(act, first["v2"], tt)
                copy_result(v2[:, tt, :], R_V + tt)
            act.wait_ge(at.cqp, 1)
            act.activation(cq, bank[7][:, 0:32].rearrange("p (t n) -> p t n", t=T), ACT.Copy).then_inc(at.cq, 1)
            act.wait_ge(b2.lruT, 4)

            def copy_c(hh):
                act.wait_ge(at.ckp, hh + 1)
                act.activation(nck[hh % 2], bank[6 + hh % 2][:, :], ACT.Copy, scale=-1.0).then_inc(at.ck, 1)

            def exp2(g):
                n = P * (g % 4 + 1)
                act.wait_ge(at.negmax, 64 + g + 1)
                act.activation(p2[g % 2][:, 0:n], lg2[g % 2][:, 0:n], ACT.Exp, bias=negmax[:, g % 2:g % 2 + 1],
                               accum_out=rs2[:, g % 4:g % 4 + 1]).then_inc(at.exp, 1)

            copy_c(0)
            exp2(0)
            for g in range(32):
                if g < 31:
                    exp2(g + 1)
                n = P * (g % 4 + 1)
                act.wait_ge(at.at, 32 + g + 1)
                act.activation(p2T[:, 0:n], bank[2 + g % 2][:, 0:n], ACT.Copy).then_inc(at.aT, 1)
                if g % 4 == 1 and g < 28:
                    copy_c(g // 4 + 1)
            turned("att2", 4)
            norm_root()
            turned("rms1")
            mixture(2)
            norm_root()

        @block.vector
        def _(dve):
            link = waits(dve, dve_step)
            norms = [0]

            def root():
                norms[0] += 1
                dve.wait_ge(norm_std, norms[0])
                link(dve.reciprocal(rstd, rstd))

            def layer_norm(which, done, count0):
                for tt in range(T):
                    for n in range(2):
                        ins = dve.bn_stats(out=stats[:, n, :], in_=h[:, tt, 512 * n:512 * n + 512])
                        link(ins)
                    link(dve.bn_aggr(out=mv[:, tt, :], in_=stats))
                dve.tensor_scalar(rstd, mv[:, :, 1], 1e-5, None, ALU.add).then_inc(norm_var, 1)
                root()
                dve.wait_ge(which, 32)
                for tt in range(T):
                    link(dve.tensor_scalar(h[:, tt, :], h[:, tt, :], mv[:, tt, 0:1], rstd[:, tt:tt + 1],
                                           ALU.subtract, ALU.mult))
                    link(dve.tensor_tensor(h[:, tt, :], h[:, tt, :], lnp[:, 0:D], ALU.mult))
                    dve.tensor_tensor(h[:, tt, :], h[:, tt, :], lnp[:, D:2 * D], ALU.add).then_inc(done, 1)
                dve.wait_ge(done, count0 + T)

            def rms_norm(gain, par_sem, dst, done, count0, eps):
                for tt in range(T):
                    link(dve.tensor_tensor_reduce(out=dst[:, tt, :], in0=h[:, tt, :], in1=h[:, tt, :], scale=1.0,
                                                  scalar=0.0, op0=ALU.mult, op1=ALU.add,
                                                  accum_out=rstd[:, tt:tt + 1]))
                link(dve.tensor_scalar(rstd, rstd, 1.0 / D, eps, ALU.mult, ALU.add))
                dve.sem_inc(norm_var, 1)
                root()
                dve.wait_ge(par_sem, 16)
                for tt in range(T):
                    dve.scalar_tensor_tensor(out=dst[:, tt, :], in0=h[:, tt, :], scalar=rstd[:, tt:tt + 1], in1=gain,
                                             op0=ALU.mult, op1=ALU.mult).then_inc(done, 1)
                dve.wait_ge(done, count0 + T)

            def residual(u, alpha):
                for n in range(2):
                    for tt in range(T):
                        wait_tile(dve, u + 2 * n, tt)
                        hs = h[:, tt, 512 * n:512 * n + 512]
                        link(dve.scalar_tensor_tensor(out=hs, in0=hs, scalar=alpha, in1=bank[4 * n + tt][:, :],
                                                      op0=ALU.mult, op1=ALU.add))

            dve.memset(zeros[:, :], 0.0).then_inc(zero_ready, 1)
            dve.wait_ge(par.lam, 64)
            for a in range(2):
                link(dve.tensor_tensor(lamv[:, 2 * a, :], lamv[:, 2 * a, :], lamv[:, 2 * a + 1, :], ALU.mult))
                link(dve.tensor_reduce(lam[:, a:a + 1], lamv[:, 2 * a, :], AX, ALU.add))
            dve.sem_inc(at.lam_in, 1)
            dve.wait_ge(at.lam_ex, 1)
            link(dve.tensor_tensor(lam[:, 2:3], lam[:, 1:2], lam[:, 0:1], ALU.subtract))
            link(dve.tensor_scalar(lam[:, 3:4], lam[:, 2:3], -LAMBDA_INIT, None, ALU.add))
            dve.wait_ge(par.subg, 16)
            link(dve.tensor_scalar(subg, subg, 1.0 - LAMBDA_INIT, None, ALU.mult))
            dve.wait_ge(const_loaded, 16)
            dve.wait_ge(par.rope, 16)

            def rope(cc):
                dve.wait_ge(at.perm, cc + 1)
                pair, n = cc // 4, cc % 4
                dst = (qT if n < 2 else kT)[(2 * pair + n % 2) % 4]
                dve.tensor_tensor(rtmp, bank[cc % 2][:, :], ropes, ALU.mult)
                link(dve.tensor_tensor(dst, raw[cc % 2], ropec, ALU.mult))
                dve.tensor_tensor(dst, dst, rtmp, ALU.add).then_inc(at.rope, 1)
                dve.wait_ge(at.rope, cc + 1)

            def maxima(g):
                qb = g % 4
                for m in range(2):
                    dve.wait_ge(at.sc, 2 * g + m + 1)
                    sc = bank[2 + 2 * (g % 2) + m]
                    link(dve.tensor_tensor(sc[:, P * qb:P * qb + P], sc[:, P * qb:P * qb + P], causal, ALU.add))
                    link(dve.tensor_reduce(mx[:, m:m + 1], sc[:, 0:P * (qb + 1)], AX, ALU.max))
                    dve.tensor_scalar(negmax[:, m:m + 1], mx[:, m:m + 1], -0.125, None, ALU.mult).then_inc(at.negmax, 1)

            def combine(g):
                n = P * (g % 4 + 1)
                dve.wait_ge(at.exp, 2 * g + 2)
                link(dve.reciprocal(rr, rs))
                link(dve.tensor_tensor(rr[:, 1:2], rr[:, 1:2], lam[:, 3:4], ALU.mult))
                a = abuf[g % 2][:, 0:n]
                link(dve.tensor_scalar(a, prob[0][:, 0:n], rr[:, 0:1], None, ALU.mult))
                dve.scalar_tensor_tensor(out=a, in0=prob[1][:, 0:n], scalar=rr[:, 1:2], in1=a,
                                         op0=ALU.mult, op1=ALU.add).then_inc(at.a, 1)
                dve.wait_ge(at.a, g + 1)

            for step in range(5 * 8):
                if step >= 8:
                    maxima(step - 8)
                if step % 2 == 0 and 1 <= step // 2 <= 16:
                    rope(step // 2 - 1)
                if step >= 8:
                    combine(step - 8)
            dve.wait_ge(at.o, 32)
            dve.tensor_scalar(orstd, sumsq, 1.0 / P, 1e-5, ALU.mult, ALU.add).then_inc(at.var, 1)
            dve.wait_ge(at.std, 1)
            link(dve.reciprocal(orstd, orstd))
            for tt in range(T):
                for hh in range(8):
                    oo = o1[:, tt, P * hh:P * hh + P]
                    ins = dve.scalar_tensor_tensor(out=oo, in0=oo, scalar=orstd[:, tt, hh:hh + 1], in1=subg,
                                                   op0=ALU.mult, op1=ALU.mult)
                ins.then_inc(tiles_written, 1)
            residual(first["wo"], ALPHA)
            layer_norm(par.ln0, tiles_written, turns["mix0"].src0)

            def mixture(l):
                m = moe[l]
                main = m.main()
                F = m.F
                dve.memset(gpad, -BIG)
                dve.memset(zero32, 0.0)
                link(dve.memset(pos, -1.0))
                dve.wait_ge(routing.router_loaded, 64 * l + (64 if l < 2 else 112))
                dve.wait_ge(routing.logits, l + 1)
                link(dve.tensor_tensor(logit, RT[:, 0:144].rearrange("p (t n) -> p t n", t=T), over_tiles(rbias, 36),
                                       ALU.add))
                link(dve.tensor_copy(gpad[:, :, 0:NG], logit[:, :, 0:NG]))

                def best(values, eight, at_):
                    for tt in range(T):
                        ins = dve.max(out=eight[:, tt, :], in_=values[:, tt, :])
                    link(ins)
                    for tt in range(T):
                        ins = dve.max_index(out=top8[:, at_ + tt, :], in_max=eight[:, tt, :], in_values=values[:, tt, :])
                    link(ins)

                best(gpad, g8, 0)
                link(dve.tensor_copy(tokf[:, 60:64], top8[:, 0:T, 0]))
                link(dve.tensor_tensor(emask, over_tiles(con[:, C_GRP:C_GRP + E], E), over_last(tokf[:, 60:64], E),
                                       ALU.is_equal))
                link(dve.tensor_tensor(em, logit[:, :, NG:NG + E], emask, ALU.mult))
                link(dve.tensor_scalar(emask, emask, BIG, -BIG, ALU.mult, ALU.add))
                link(dve.tensor_tensor(em, em, emask, ALU.add))
                best(em, e8, T)
                dve.tensor_copy(tokf[:, 52:56], top8[:, T:2 * T, 0])
                link(dve.tensor_copy(tokf[:, 56:60], top8[:, T:2 * T, 1]))
                expert_row = over_tiles(con[:, C_IO:C_IO + E], E)
                dve.tensor_tensor(hot1, expert_row, over_last(tokf[:, 52:56], E), ALU.is_equal)
                link(dve.tensor_tensor(hot2, expert_row, over_last(tokf[:, 56:60], E), ALU.is_equal))
                dve.tensor_tensor(hots, hot1, hot2, ALU.add).then_inc(routing.onehots, 1)
                dve.tensor_tensor(tokf[:, 0:16].rearrange("p (t n) -> p t n", t=T), gpad[:, :, 0:NG],
                                  over_last(g8[:, :, 0], NG), ALU.subtract)
                link(dve.tensor_tensor(tokf[:, 16:20], e8[:, :, 1], e8[:, :, 0], ALU.subtract))
                dve.sem_inc(routing.exp_in, 1)
                dve.wait_ge(routing.onehots, l + 1)
                dve.wait_ge(routing.ranks, l + 1)
                dve.tensor_copy(ovdiff, CT[:, 128:160])
                link(dve.tensor_copy(rank, CT[:, 0:128].rearrange("p (t n) -> p t n", t=T)))
                link(dve.scalar_tensor_tensor(out=rowE, in0=rank, scalar=float(MAIN), in1=hots,
                                              op0=ALU.is_lt, op1=ALU.mult))
                link(dve.scalar_tensor_tensor(out=rowE, in0=rank, scalar=1.0, in1=rowE, op0=ALU.add, op1=ALU.mult))
                link(dve.tensor_scalar(pos[:, :, 0:E], rowE, -1.0, None, ALU.add))
                slots = over_tiles(con[:, C_SLOT:C_SLOT + BLK], BLK)

                def select(buf, e):
                    for n in range(2):
                        ins = dve.tensor_tensor(sel[buf][:, :, BLK * n:BLK * n + BLK], slots,
                                                pos[:, :, bass.ds(e + n, 1)].to_broadcast([P, T, BLK]), ALU.is_equal)
                    ins.then_inc(main.sel, 1)

                def copy_rows(b, buf, half, count, width):
                    dve.wait_ge(b.xt, b.x0 + count)
                    dve.tensor_copy(xgT[buf][:, 4 * half:4 * half + 4, 0:width],
                                    XT[half][:, :].rearrange("p (k n) -> p k n", k=4)[:, :, 0:width])\
                        .then_inc(b.xT, 1)

                select(0, 0)
                select(1, 2)
                copy_rows(main, 0, 0, 1, P)
                copy_rows(main, 0, 1, 2, P)
                nth = len(rank_thresholds())
                over = ovcmp[:, 0:nth, :]
                link(dve.tensor_tensor(over, ovdiff.unsqueeze(1).to_broadcast([P, nth, E]),
                                       over_last(con[:, C_TH:C_TH + nth], E), ALU.is_gt))
                link(dve.tensor_reduce(nblk, over.rearrange("p k n -> p n k"), AX, ALU.add))
                link(dve.tensor_tensor_scan(ovend, nblk, zero32, 0.0, ALU.add, ALU.add))
                link(dve.tensor_tensor(ovdiff, ovend, nblk, ALU.subtract))
                link(dve.tensor_scalar(ovdiff, ovdiff, float(BLK), float(E * BLK - MAIN), ALU.mult, ALU.add))
                link(dve.scalar_tensor_tensor(out=ovdiff, in0=con[:, C_IO:C_IO + E], scalar=-float(BLK), in1=ovdiff,
                                              op0=ALU.mult, op1=ALU.add))
                link(dve.scalar_tensor_tensor(out=rowE, in0=rank, scalar=float(MAIN), in1=over_tiles(ovdiff, E),
                                              op0=ALU.is_ge, op1=ALU.mult))
                link(dve.tensor_tensor(rowE, rowE, rank, ALU.add))
                link(dve.scalar_tensor_tensor(out=rowE, in0=expert_row, scalar=float(BLK), in1=rowE,
                                              op0=ALU.mult, op1=ALU.add))
                dve.tensor_tensor(hot1, hot1, rowE, ALU.mult)
                dve.tensor_tensor(hot2, hot2, rowE, ALU.mult)
                link(dve.scalar_tensor_tensor(out=rowA, in0=rowE, scalar=1.0, in1=hots, op0=ALU.add, op1=ALU.mult))
                dve.tensor_reduce(tokf[:, 44:48], hot1, AX, ALU.add)
                dve.tensor_reduce(tokf[:, 48:52], hot2, AX, ALU.add)
                link(dve.tensor_scalar(rowA, rowA, -1.0, None, ALU.add))
                dve.tensor_copy(idx[:, :], tokf[:, 44:52])
                link(dve.tensor_tensor(ovcmp[:, 0:OVF, :], ovend.unsqueeze(1).to_broadcast([P, OVF, E]),
                                       over_last(con[:, C_J:C_J + OVF], E), ALU.is_le))
                link(dve.tensor_reduce(ovf[:, 0:OVF], ovcmp[:, 0:OVF, :], AX, ALU.add))
                link(dve.tensor_scalar(ovf[:, 0:OVF], ovf[:, 0:OVF], float(E - 1), None, ALU.min))
                dve.tensor_copy(ovi[:, 0:OVF], ovf[:, 0:OVF])
                dve.tensor_copy(ovi[:, 16:17], ovend[:, E - 1:E]).then_inc(routing.indices, 1)
                dve.wait_ge(routing.exp_out, l + 1)
                dve.tensor_reduce(tokf[:, 40:44], tokf[:, 20:36].rearrange("p (t n) -> p t n", t=T), AX, ALU.add)
                link(dve.tensor_scalar(tokf[:, 16:20], tokf[:, 36:40], 1.0, None, ALU.add))
                link(dve.tensor_tensor(tokf[:, 40:44], tokf[:, 40:44], tokf[:, 16:20], ALU.mult))
                link(dve.reciprocal(wts[:, 0, :], tokf[:, 40:44]))
                link(dve.tensor_tensor(wts[:, 1, :], wts[:, 0, :], tokf[:, 36:40], ALU.mult))

                def expert(b, j, ahead):
                    dve.wait_ge(b.sg, b.n0 + j + 1)
                    dve.tensor_tensor(hg[:, 0:F], sg[:, 0:F], GU[BLK:P, 0:F], ALU.mult).then_inc(b.hg, 1)
                    if ahead is not None:
                        ahead()
                    dve.wait_ge(b.ht, b.n0 + j + 1)
                    dve.tensor_copy(hgT[:, 0:F // 2], HT[:, 0:F // 2]).then_inc(b.hT, 1)

                def body(i, s):
                    pair, j = s // 2, TURN * i + s
                    expert(main, j, lambda: copy_rows(main, (pair + 1) % 2, s % 2, j + 3, P))
                    if s % 2:
                        select(pair % 2, j + 3)
                over_blocks(dve, body)
                dve.wait_ge(routing.indices, m.l + 1)
                count = dve.value_load(ovi[0:1, 16:17], min_val=0, max_val=OVF)
                with dve.If(count > 0):
                    with dve.Fori(0, count) as j:
                        e = dve.value_load(ovi[0:1, bass.ds(j, 1)], min_val=0, max_val=E - 1)
                        dve.tensor_scalar(oslot, rowA[:, :, bass.ds(e, 1)], con[:, bass.ds(C_OB + j, 1)], None,
                                          ALU.subtract).then_inc(m.ov.slot, 1)
                        dve.wait_ge(m.ov.slot, j + 1)
                        dve.tensor_tensor(sel[0][:, :, 0:BLK], slots, over_last(oslot, BLK), ALU.is_equal)\
                            .then_inc(m.ov.sel, 1)
                        copy_rows(m.ov, 0, 0, 2 * j + 1, BLK)
                        copy_rows(m.ov, 0, 1, 2 * j + 2, BLK)
                        expert(m.ov, j, None)

                for tt in range(T):
                    dve.wait_ge([routing.gathered0, routing.gathered1][tt % 2], 64 * l + 32 * (tt // 2 + 1))
                    y = ygat[tt % 2]
                    link(dve.tensor_scalar(y[1], y[1], wts[:, 1, tt:tt + 1], None, ALU.mult))
                    link(dve.scalar_tensor_tensor(out=y[0], in0=y[0], scalar=wts[:, 0, tt:tt + 1], in1=y[1],
                                                  op0=ALU.mult, op1=ALU.add))
                    link(dve.scalar_tensor_tensor(out=h[:, tt, :], in0=h[:, tt, :], scalar=ALPHA if l < 2 else 1.0,
                                                  in1=y[0], op0=ALU.mult, op1=ALU.add))
                    dve.sem_inc(routing.summed, 1)

            mixture(0)
            layer_norm(par.ln1, tiles_written, turns["ffn0"].src0)
            link(dve.memset(uT[:, :, 0:PAD], 0.0))
            for i in range(2):
                link(dve.memset(win[i][:, :, 0:PAD], 0.0))
            for g in range(4):
                dve.wait_ge(po.u, 2 * g + 2)
                src = uT[:, 2 * g:2 * g + 2, :]
                width = 1
                for d in range(g + 1):
                    dst = win[d % 2]
                    link(dve.tensor_tensor(dst[:, :, PAD:], src[:, :, PAD:], src[:, :, PAD - width:PAD + S - width],
                                           ALU.add))
                    src, width = dst, 2 * width
                pg = pT[:, 2 * g:2 * g + 2, :]
                u_ = uT[:, 2 * g:2 * g + 2, PAD:]
                link(dve.scalar_tensor_tensor(out=pg, in0=src[:, :, PAD:], scalar=1.0 / width, in1=u_,
                                              op0=ALU.mult, op1=ALU.subtract))
                for k in range(2):
                    link(dve.tensor_tensor(pg[:, k, 0:PAD], src[:, k, PAD:2 * PAD],
                                           con[:, C_INV + PAD * g:C_INV + PAD * g + PAD], ALU.mult))
                    link(dve.tensor_tensor(pg[:, k, 0:PAD], pg[:, k, 0:PAD], u_[:, k, 0:PAD], ALU.subtract))
                dve.sem_inc(po.p, 1)
            residual(first["pout"], ALPHA)
            layer_norm(par.ln2, tiles_written, turns["mix1"].src0)
            mixture(1)
            layer_norm(par.ln3, ln3_done, 0)
            rms_norm(lnp[:, 0:D], par.rms0, hn, tiles_written, turns["rms0"].src0, 1e-6)
            def log1p(y, w, acc):
                link(dve.tensor_scalar(w, y, 2.0, None, ALU.add))
                link(dve.reciprocal(w, w))
                link(dve.tensor_tensor(y, y, w, ALU.mult))
                link(dve.tensor_tensor(w, y, y, ALU.mult))
                link(dve.tensor_scalar(acc, w, 1.0 / (2 * SERIES + 1), None, ALU.mult))
                for n in range(SERIES - 1, -1, -1):
                    link(dve.scalar_tensor_tensor(out=acc, in0=acc, scalar=1.0 / (2 * n + 1), in1=w if n else y,
                                                  op0=ALU.add, op1=ALU.mult))

            dve.wait_ge(par.conv, 128)
            lm, sy, sw, sacc, sp8 = convp[:, 28:32], spl[:, 0:4], spl[:, 4:8], spl[:, 8:12], spl[:, 12:16]
            link(dve.scalar_tensor_tensor(out=sy, in0=lm, scalar=-1.0, in1=lm, op0=ALU.mult, op1=ALU.min))
            dve.sem_inc(b2.sp_in, 1)
            dve.wait_ge(b2.sp_e, 1)
            log1p(sy, sw, sacc)
            link(dve.tensor_scalar(sp8, lm, -1.0, 0.0, ALU.mult, ALU.max))
            link(dve.scalar_tensor_tensor(out=sp8, in0=sacc, scalar=2.0, in1=sp8, op0=ALU.mult, op1=ALU.add))
            link(dve.tensor_scalar(sp8, sp8, 8.0, None, ALU.mult))
            for ch in range(4):
                dve.wait_ge(b2.copied, R_REC + ch + 1)
                link(dve.tensor_scalar(bx[:, ch, :], be[:, ch, :], taps[:, 3, ch:ch + 1], convp[:, 16 + ch:17 + ch],
                                       ALU.mult, ALU.add))
                for lag in range(1, 4):
                    ins = dve.scalar_tensor_tensor(out=bx[:, ch, lag:S], in0=be[:, ch, 0:S - lag],
                                                   scalar=taps[:, 3 - lag, ch:ch + 1], in1=bx[:, ch, lag:S],
                                                   op0=ALU.mult, op1=ALU.add)
                    if lag < 3:
                        link(ins)
                ins.then_inc(b2.conv, 1)
            dve.wait_ge(b2.copied, R_F + 1)
            dve.scalar_tensor_tensor(out=fb[1], in0=fb[0], scalar=-1.0, in1=fb[0], op0=ALU.mult, op1=ALU.min)\
                .then_inc(b2.f_in, 1)
            dve.wait_ge(b2.f_e, 1)
            log1p(fb[1], fb[2], fb[3])
            link(dve.tensor_scalar(fb[0], fb[0], 0.0, None, ALU.min))
            link(dve.scalar_tensor_tensor(out=fb[1], in0=fb[3], scalar=-2.0, in1=fb[0], op0=ALU.mult, op1=ALU.add))
            link(dve.memset(fb[2], 0.0))
            dve.tensor_tensor_scan(fb[0], fb[1], fb[2], 0.0, ALU.add, ALU.add).then_inc(b2.c, 1)
            for ch in range(4):
                dve.wait_ge(b2.copied, R_LRU + 2 * ch + 2)
                dve.tensor_scalar(br[:, ch, :], br[:, ch, :], sp8[:, ch:ch + 1], None, ALU.mult)\
                    .then_inc(b2.decay, 1)
                link(dve.tensor_tensor(bi[:, ch, :], bi[:, ch, :], bx[:, ch, :], ALU.mult))
            for ch in range(4):
                dve.wait_ge(b2.tau, ch + 1)
                link(dve.tensor_scalar(bx[:, ch, :], br[:, ch, :], 1.0, None, ALU.add))
                link(dve.reciprocal(bx[:, ch, :], bx[:, ch, :]))
                dve.scalar_tensor_tensor(out=br[:, ch, :], in0=br[:, ch, :], scalar=2.0, in1=bx[:, ch, :],
                                         op0=ALU.mult, op1=ALU.mult).then_inc(b2.m2, 1)
            for ch in range(4):
                dve.wait_ge(b2.mult, ch + 1)
                link(dve.tensor_tensor(bi[:, ch, :], bi[:, ch, :], br[:, ch, :], ALU.mult))
                link(dve.tensor_tensor_scan(bx[:, ch, :], be[:, ch, :], bi[:, ch, :], 0.0, ALU.mult, ALU.add))
            dve.wait_ge(units_used, first["v2"] + 2)
            for ch in range(4):
                dve.tensor_tensor(hT[:, 4 + ch, :], bx[:, ch, :], bg[:, ch, :], ALU.mult).then_inc(b2.lruT, 1)
            dve.wait_ge(b2.lruT, 4)
            dve.wait_ge(at.cq, 1)

            def logits2(g):
                hh, qb = g // 4, g % 4
                n, lg = P * (qb + 1), lg2[g % 2]
                dve.wait_ge(at.sc, 64 + g + 1)
                dve.wait_ge(at.ck, hh + 1)
                link(dve.scalar_tensor_tensor(out=lg[:, 0:n], in0=bank[g % 2][:, 0:n], scalar=cq[:, qb, hh:hh + 1],
                                              in1=nck[hh % 2][:, 0:n], op0=ALU.add, op1=ALU.add))
                link(dve.tensor_tensor(lg[:, P * qb:n], lg[:, P * qb:n], causal, ALU.add))
                link(dve.tensor_reduce(mx[:, g % 2:g % 2 + 1], lg[:, 0:n], AX, ALU.max))
                dve.tensor_scalar(negmax[:, g % 2:g % 2 + 1], mx[:, g % 2:g % 2 + 1], -1.0, None, ALU.mult)\
                    .then_inc(at.negmax, 1)

            def out2(g):
                hh, qb = g // 4, g % 4
                dve.wait_ge(at.av, 32 + g + 1)
                q = slice(g % 4, g % 4 + 1)
                link(dve.reciprocal(rr2[:, q], rs2[:, q]))
                dve.tensor_scalar(att2[:, qb, 64 * hh:64 * hh + 64], bank[4 + g % 2][:, 0:64], rr2[:, q], None,
                                  ALU.mult).then_inc(at.o, 1)

            logits2(0)
            for g in range(32):
                if g < 31:
                    logits2(g + 1)
                if g >= 1:
                    out2(g - 1)
            out2(31)
            dve.wait_ge(at.o, 64)
            dve.sem_inc(tiles_written, T)
            residual(first["out2"], 1.0)
            rms_norm(lnp[:, 0:D], par.rms1, hn, tiles_written, turns["rms1"].src0, 1e-6)
            mixture(2)
            rms_norm(lnp[:, D:2 * D], par.rms2, hn, out_ready, 0, 1e-6)

        @block.gpsimd
        def _(pool):
            def bcast(dst, src, s, n):
                pool.dma_start(dst, src.to_broadcast([P, n])).then_inc(s, 16)

            bcast(subg, t["attn_sub_g"], par.subg, 128)
            for i, n in enumerate(("attn_lq1", "attn_lk1", "attn_lq2", "attn_lk2")):
                bcast(lamv[:, i, :], t[n], par.lam, 64)

            def load_norm(s, layer, half, after, count):
                pool.wait_ge(after, count)
                bcast(lnp[:, 0:D], t["ln_g"][layer, half:half + 1, :], s, D)
                bcast(lnp[:, D:2 * D], t["ln_b"][layer, half:half + 1, :], s, D)

            load_norm(par.ln0, 0, 0, at.rope, 16)

            def mixture(l, before):
                m = moe[l]
                main = m.main()
                pool.wait_ge(tiles_written, turns[before].src_all)
                pool.dma_start(wr[:, :, 0:NG], router_g[l].rearrange("(k p) n -> p k n", p=P))\
                    .then_inc(routing.router_loaded, 16)
                if l < 2:
                    pool.dma_start(wr[:, :, NG:NG + E], t["moe_w_exp_router"][l].rearrange("(k p) n -> p k n", p=P))\
                        .then_inc(routing.router_loaded, 16)
                else:
                    for g in range(NG):
                        pool.dma_start(wr[:, :, NG + 8 * g:NG + 8 * g + 8],
                                       t["w_inner_2"][0, g].rearrange("(k p) n -> p k n", p=P))\
                            .then_inc(routing.router_loaded, 16)
                bcast(rbias[:, 0:NG], router_gb[l], routing.router_loaded, NG)
                bcast(rbias[:, NG:NG + E], router_eb[l], routing.router_loaded, E)
                if l == 0:
                    pool.wait_ge(rows_zeroed, 16)
                pool.wait_ge(routing.indices, m.l + 1)
                for s in range(2):
                    pool.wait_ge(main.y_stored[s], main.store0[s] + 32 * E // 2)
                count = pool.value_load(ovi[0:1, 16:17], min_val=0, max_val=OVF)
                with pool.If(count > 0):
                    pool.wait_ge(m.ov.y_stored[0], 32 * count)
                for tt in range(T):
                    if tt >= 2:
                        pool.wait_ge(routing.summed, T * l + tt - 1)
                    for k in range(2):
                        pool.indirect_dma_start(
                            out=ygat[tt % 2][k], out_offset=None, in_=y_rows,
                            in_offset=bass.IndirectOffsetOnAxis(ap=idx[:, T * k + tt:T * k + tt + 1], axis=0))\
                            .then_inc([routing.gathered0, routing.gathered1][tt % 2], 16)

            load_norm(par.ln1, 0, 1, tiles_written, turns["mix0"].src_all)
            mixture(0, "mix0")
            load_norm(par.ln2, 1, 0, tiles_written, turns["ffn0"].src_all)
            pool.dma_start(pscale, t["pool_scale"][0].rearrange("(k p) -> p k", p=P),
                           allow_slow_non_contiguous=True).then_inc(par.pscale, 16)
            load_norm(par.ln3, 1, 1, tiles_written, turns["mix1"].src_all)
            mixture(1, "mix1")
            pool.wait_ge(ln3_done, T)
            bcast(lnp[:, 0:D], t["mix_norm_2"], par.rms0, D)
            def vector(dst, src, s):
                pool.dma_start(dst, src.rearrange("a (c p) -> p (a c)", p=P), allow_slow_non_contiguous=True)\
                    .then_inc(s, 16)

            for i in range(4):
                vector(taps[:, i, :], t["conv_w_2"][0, i:i + 1, :], par.conv)
            vector(convp[:, 16:20], t["conv_b_2"], par.conv)
            vector(convp[:, 20:24], t["b_a_2"].rearrange("l n i -> l (n i)"), par.conv)
            vector(convp[:, 24:28], t["b_x_2"].rearrange("l n i -> l (n i)"), par.conv)
            vector(convp[:, 28:32], t["lru_lambda_2"], par.conv)
            pool.dma_start(wf, t["w_in_2"][0][:, 1536:1544].rearrange("(k p) n -> p k n", p=P))\
                .then_inc(par.wf, 16)
            pool.dma_start(bfg, t["b_forget_2"].rearrange("a n -> n a"), allow_slow_non_contiguous=True)\
                .then_inc(par.bf, 16)
            for a, n in enumerate(("w_a_2", "w_x_2")):
                for b in range(2):
                    pool.dma_start(wab[64 * b:64 * b + 64, a, :, :],
                                   t[n][0].rearrange("(c b) i j -> b i c j", b=2)[b]).then_inc(par.wab, 16)
            pool.wait_ge(at.ck, 8)
            bcast(lnp[:, 0:D], t["ffn_norm_2"], par.rms1, D)
            bcast(lnp[:, D:2 * D], t["final_norm_2"].unsqueeze(0), par.rms2, D)
            mixture(2, "rms1")


_INS = ["x", "attn_w_qkv", "attn_w_o", "attn_lq1", "attn_lk1", "attn_lq2", "attn_lk2", "attn_sub_g", "pool_w_in",
        "pool_w_grp", "pool_scale", "pool_w_out", "ln_g", "ln_b", "moe_w_grp_router", "moe_b_grp_router",
        "moe_w_exp_router", "moe_b_exp_router", "moe_w_gate", "moe_w_up", "moe_w_down", "mix_norm_2", "w_in_2",
        "b_forget_2", "conv_w_2", "conv_b_2", "w_a_2", "b_a_2", "w_x_2", "b_x_2", "lru_lambda_2", "w_out_2",
        "ffn_norm_2", "w_group_2", "b_group_2", "w_inner_2", "b_inner_2", "w_gate_2", "w_up_2", "w_down_2",
        "final_norm_2"]


def constants():
    import numpy as np

    p = np.arange(P)
    con = np.zeros((P, C_W), np.float32)
    con[:, C_ID:C_ID + P] = np.eye(P)
    con[:, C_TRI:C_TRI + P] = p[:, None] < p[None, :]
    con[:, C_ONE:C_ONE + P] = 1
    con[:, C_CAUS:C_CAUS + P] = np.where(p[None, :] <= p[:, None], 0, -BIG)
    for q in range(P):
        if q % 64 < 16:
            con[q // 64 * 64 + (q % 64 + 8) % 16, C_ROPE + q] = 1
    con[:, C_IO:C_IO + E] = np.arange(E)
    con[:, C_J:C_J + 16] = np.arange(16)
    con[:, C_OB:C_OB + 16] = BLK * (E + np.arange(16))
    con[:, C_TH:C_TH + len(rank_thresholds())] = rank_thresholds()
    con[:, C_SLOT:C_SLOT + BLK] = np.arange(BLK)
    con[:, C_GRP:C_GRP + E] = np.arange(E) // (E // NG)
    for g in range(4):
        con[:, C_INV + 16 * g:C_INV + 16 * g + 16] = np.float32(1) / np.minimum(np.arange(1, 17), 2 ** (g + 1))
    inv = np.float32(500000.0) ** (-np.arange(0, 16, 2, dtype=np.float32) / np.float32(16))
    ang = np.arange(S, dtype=np.float32)[:, None] * inv[None, :]
    cos, sin = np.cos(ang).T, np.sin(ang).T
    rope = np.zeros((P, 2, S), np.float32)
    rope[:, 0] = 1
    for m in range(2):
        b = 64 * m
        rope[b:b + 8, 0], rope[b + 8:b + 16, 0] = cos, cos
        rope[b:b + 8, 1], rope[b + 8:b + 16, 1] = -sin, sin
    return con, rope.reshape(P, 2 * S)


def kernel(**inputs):
    import numpy as _np
    import concourse.bacc as _bacc
    from concourse import mybir as _mybir
    from concourse.bass_utils import run_bass_kernel_spmd as _run

    nc = _bacc.Bacc("TRN2", target_bir_lowering=False, num_devices=1)
    arrays, aps = {}, {}
    con, rope = constants()
    for name, a in [(n, inputs[n]) for n in _INS] + [("con", con), ("rope", rope)]:
        a = _np.ascontiguousarray(a)
        arrays[f"in_{name}_dram"] = a
        aps[name] = nc.dram_tensor(f"in_{name}_dram", a.shape, _mybir.dt.from_np(a.dtype), kind="ExternalInput").ap()
    aps["out"] = nc.dram_tensor("out_0_dram", (1, S, D), _mybir.dt.float32, kind="ExternalOutput").ap()
    program(nc, aps)
    r = _run(nc, [arrays], core_ids=[0])
    return r.results[0]["out_0_dram"]
```
